# Optimizing a Trainium2 kernel written in Bass

```python
import math
import jax, jax.numpy as jnp
from jax import lax
import numpy as np

D_MODEL = 1024
BATCH = 1
SEQ = 256
DEPTH = 1

CHUNK = 64
PLE_DIM = 256
RMS_EPS = 1e-6
LN_EPS = 1e-5

SGU_HEADS = 8
SGU_HEAD_DIM = 128
SGU_WIDTH = SGU_HEADS * SGU_HEAD_DIM
SGU_LEN = 128

SSM_HEADS = 16
SSM_HEAD_DIM = 64
SSM_INNER = SSM_HEADS * SSM_HEAD_DIM
SSM_GROUPS = 4
SSM_STATE = 128
SSM_CONV = 4
SSD_CHUNK = 128
SSM_CONV_DIM = SSM_INNER + 2 * SSM_GROUPS * SSM_STATE

N_EXPERTS = 32
TOP_K = 4
D_FF_EXPERT = 1024
SWIGLU_LIMIT = 7.0
SWIGLU_ALPHA = 1.702
MOE_BLOCK = 256

OFF_U = 0
OFF_V = OFF_U + SGU_WIDTH
OFF_Z = OFF_V + SGU_WIDTH
OFF_XBC = OFF_Z + SSM_INNER
OFF_DT = OFF_XBC + SSM_CONV_DIM
OFF_GA = OFF_DT + SSM_HEADS
OFF_GB = OFF_GA + D_MODEL
IN_PROJ_DIM = OFF_GB + D_MODEL

kernel_name = "hybrid_sgu_ssd_moe_streaming_block"

def rms_norm(x, g):
    xf = x.astype(jnp.float32)
    y = xf * lax.rsqrt(jnp.mean(xf * xf, axis=-1, keepdims=True) + RMS_EPS)
    return (y * g.astype(jnp.float32)).astype(x.dtype)

def layer_norm(x, g, b):
    xf = x.astype(jnp.float32)
    mu = jnp.mean(xf, axis=-1, keepdims=True)
    var = jnp.mean(jnp.square(xf - mu), axis=-1, keepdims=True)
    y = (xf - mu) * lax.rsqrt(var + LN_EPS)
    return (y * g.astype(jnp.float32) + b.astype(jnp.float32)).astype(x.dtype)

def sgu_branch(uv, ln_g, ln_b, w_s, b_s):
    bsz, seq, _ = uv.shape
    uv = jax.nn.gelu(uv, approximate=False)
    u, v = jnp.split(uv, 2, axis=-1)
    v = layer_norm(v, ln_g, ln_b)
    v = v.reshape(bsz, seq // SGU_LEN, SGU_LEN, SGU_HEADS, SGU_HEAD_DIM)
    pos = jnp.arange(SGU_LEN)
    allowed = (pos[None, :] // CHUNK) <= (pos[:, None] // CHUNK)
    w = jnp.where(allowed[None], w_s, jnp.zeros_like(w_s))
    mixed = jnp.einsum("gts,bnsgc->bntgc", w, v) + b_s.T[:, :, None]
    return u * mixed.reshape(bsz, seq, SGU_WIDTH)

def causal_depthwise_conv(x, w, b):
    y = lax.conv_general_dilated(
        x, w[:, None, :].astype(x.dtype), window_strides=(1,),
        padding=[(SSM_CONV - 1, 0)], dimension_numbers=("NWC", "WIO", "NWC"),
        feature_group_count=x.shape[-1])
    return y + b

def ssd_scan(x, dt, a, b_mat, c_mat):
    bsz, seq = x.shape[:2]
    nc, q = seq // SSD_CHUNK, SSD_CHUNK
    g, r = SSM_GROUPS, SSM_HEADS // SSM_GROUPS
    p, n = SSM_HEAD_DIM, SSM_STATE
    xf = x.astype(jnp.float32).reshape(bsz, nc, q, g, r, p)
    dt = dt.reshape(bsz, nc, q, g, r)
    bm = b_mat.astype(jnp.float32).reshape(bsz, nc, q, g, n)
    cm = c_mat.astype(jnp.float32).reshape(bsz, nc, q, g, n)
    a_dt = (dt * a.reshape(g, r)).transpose(0, 3, 4, 1, 2)
    a_cs = jnp.cumsum(a_dt, axis=-1)
    tri = jnp.tril(jnp.ones((q, q), dtype=bool))
    seg = a_cs[..., :, None] - a_cs[..., None, :]
    decay_in = jnp.exp(jnp.where(tri, seg, -jnp.inf))
    xdt = xf * dt[..., None]
    cb = jnp.einsum("bcqgn,bcsgn->bcgqs", cm, bm)
    y_diag = jnp.einsum("bcgqs,bgrcqs,bcsgrp->bcqgrp", cb, decay_in, xdt)
    decay_to_end = jnp.exp(a_cs[..., -1:] - a_cs)
    chunk_states = jnp.einsum("bcsgn,bgrcs,bcsgrp->cbgrpn", bm, decay_to_end, xdt)
    chunk_decay = jnp.exp(a_cs[..., -1]).transpose(3, 0, 1, 2)

    def step(h, inp):
        s_c, a_c = inp
        return a_c[..., None, None] * h + s_c, h

    h0 = jnp.zeros((bsz, g, r, p, n), jnp.float32)
    _, prev_states = lax.scan(step, h0, (chunk_states, chunk_decay))
    y_off = jnp.einsum("bcqgn,cbgrpn,bgrcq->bcqgrp", cm, prev_states, jnp.exp(a_cs))
    return (y_diag + y_off).reshape(bsz, seq, SSM_HEADS, SSM_HEAD_DIM)

def mamba2_branch(z, xbc, dt_raw, conv_w, conv_b, dt_bias, a_log, d_skip, norm_w):
    bsz, seq, _ = z.shape
    xbc = jax.nn.silu(causal_depthwise_conv(xbc, conv_w, conv_b))
    xs, bm, cm = jnp.split(xbc, [SSM_INNER, SSM_INNER + SSM_GROUPS * SSM_STATE], axis=-1)
    xs = xs.reshape(bsz, seq, SSM_HEADS, SSM_HEAD_DIM)
    bm = bm.reshape(bsz, seq, SSM_GROUPS, SSM_STATE)
    cm = cm.reshape(bsz, seq, SSM_GROUPS, SSM_STATE)
    dt = jax.nn.softplus(dt_raw.astype(jnp.float32) + dt_bias.astype(jnp.float32))
    a = -jnp.exp(a_log.astype(jnp.float32))
    y = ssd_scan(xs, dt, a, bm, cm) + d_skip.astype(jnp.float32)[:, None] * xs.astype(jnp.float32)
    y = y.reshape(bsz, seq, SSM_GROUPS, SSM_INNER // SSM_GROUPS)
    y = y * jax.nn.silu(z.astype(jnp.float32)).reshape(y.shape)
    y = y * lax.rsqrt(jnp.mean(y * y, axis=-1, keepdims=True) + RMS_EPS)
    y = y.reshape(bsz, seq, SSM_INNER) * norm_w.astype(jnp.float32)
    return y.astype(z.dtype)

def moe_ffn(h, w_router, b_router, w1, b1, w2, b2):
    bsz, seq, d = h.shape
    t = h.reshape(-1, d)
    n = t.shape[0]
    logits = (t @ w_router + b_router).astype(jnp.float32)
    top_val, top_idx = lax.top_k(logits, TOP_K)
    gate = jax.nn.softmax(top_val, axis=-1)
    flat_e = top_idx.reshape(-1).astype(jnp.int32)
    flat_tok = jnp.repeat(jnp.arange(n, dtype=jnp.int32), TOP_K)
    flat_gate = gate.reshape(-1)
    nk = n * TOP_K
    order = jnp.argsort(flat_e)
    sorted_e = flat_e[order]
    counts = jnp.bincount(flat_e, length=N_EXPERTS).astype(jnp.int32)
    padded = (counts + MOE_BLOCK - 1) // MOE_BLOCK * MOE_BLOCK
    start = jnp.cumsum(counts) - counts
    pend = jnp.cumsum(padded)
    pstart = pend - padded
    rank = jnp.arange(nk, dtype=jnp.int32) - start[sorted_e]
    dest = pstart[sorted_e] + rank
    cap = (nk + MOE_BLOCK - 1) // MOE_BLOCK * MOE_BLOCK + N_EXPERTS * MOE_BLOCK
    n_blocks = cap // MOE_BLOCK
    buf_tok = jnp.zeros((cap,), jnp.int32).at[dest].set(flat_tok[order])
    buf_gate = jnp.zeros((cap,), jnp.float32).at[dest].set(flat_gate[order])
    blk_start = jnp.arange(n_blocks, dtype=jnp.int32) * MOE_BLOCK
    blk_expert = jnp.minimum(jnp.searchsorted(pend, blk_start, side="right"), N_EXPERTS - 1)
    xs = t[buf_tok].reshape(n_blocks, MOE_BLOCK, d)

    def expert_block(args):
        xb, e = args
        hid = xb @ w1[e] + b1[e]
        glu, lin = jnp.split(hid, 2, axis=-1)
        glu = jnp.minimum(glu, SWIGLU_LIMIT)
        lin = jnp.clip(lin, -SWIGLU_LIMIT, SWIGLU_LIMIT)
        act = glu * jax.nn.sigmoid(SWIGLU_ALPHA * glu) * (lin + 1)
        return act @ w2[e] + b2[e]

    ys = lax.map(expert_block, (xs, blk_expert)).reshape(cap, d)
    out = jax.ops.segment_sum(ys.astype(jnp.float32) * buf_gate[:, None], buf_tok, num_segments=n)
    return out.astype(h.dtype).reshape(bsz, seq, d)

def setup_inputs(seed: int = 0) -> dict:
    key = jax.random.key(seed)
    ks = iter(jax.random.split(key, 40))

    def nrm(shape, scale):
        return jax.random.normal(next(ks), shape, jnp.float32) * scale

    def gain(shape):
        return 1.0 + nrm(shape, 0.05)

    L = DEPTH
    dt0 = jnp.exp(jax.random.uniform(next(ks), (L, SSM_HEADS), jnp.float32)
                  * (math.log(0.1) - math.log(0.001)) + math.log(0.001))
    dt_bias = dt0 + jnp.log(-jnp.expm1(-dt0))
    a_log = jnp.log(jax.random.uniform(next(ks), (L, SSM_HEADS), jnp.float32, 1.0, 16.0))
    return {
        "x": nrm((BATCH, SEQ, D_MODEL), 1.0),
        "p": nrm((L, BATCH, SEQ, PLE_DIM), 1.0),
        "mix_norm": gain((L, D_MODEL)),
        "w_in": nrm((L, D_MODEL, IN_PROJ_DIM), D_MODEL ** -0.5),
        "sgu_ln_g": gain((L, SGU_WIDTH)),
        "sgu_ln_b": nrm((L, SGU_WIDTH), 0.02),
        "sgu_w": nrm((L, SGU_HEADS, SGU_LEN, SGU_LEN), SGU_LEN ** -0.5),
        "sgu_b": 1.0 + nrm((L, SGU_HEADS, SGU_LEN), 0.1),
        "conv_w": nrm((L, SSM_CONV, SSM_CONV_DIM), SSM_CONV ** -0.5),
        "conv_b": nrm((L, SSM_CONV_DIM), 0.02),
        "dt_bias": dt_bias,
        "a_log": a_log,
        "d_skip": 1.0 + nrm((L, SSM_HEADS), 0.1),
        "ssm_norm": gain((L, SSM_INNER)),
        "w_branch_a": nrm((L, SGU_WIDTH, D_MODEL), SGU_WIDTH ** -0.5),
        "w_branch_b": nrm((L, SSM_INNER, D_MODEL), SSM_INNER ** -0.5),
        "w_out": nrm((L, D_MODEL, D_MODEL), D_MODEL ** -0.5),
        "ffn_norm": gain((L, D_MODEL)),
        "w_router": nrm((L, D_MODEL, N_EXPERTS), D_MODEL ** -0.5),
        "b_router": nrm((L, N_EXPERTS), 0.01),
        "w1": nrm((L, N_EXPERTS, D_MODEL, 2 * D_FF_EXPERT), D_MODEL ** -0.5),
        "b1": nrm((L, N_EXPERTS, 2 * D_FF_EXPERT), 0.01),
        "w2": nrm((L, N_EXPERTS, D_FF_EXPERT, D_MODEL), D_FF_EXPERT ** -0.5),
        "b2": nrm((L, N_EXPERTS, D_MODEL), 0.01),
        "ple_norm": gain((L, D_MODEL)),
        "w_ple_gate": nrm((L, D_MODEL, D_MODEL), D_MODEL ** -0.5),
        "w_ple_proj": nrm((L, PLE_DIM, D_MODEL), PLE_DIM ** -0.5),
        "final_norm": gain((D_MODEL,)),
    }

def reference(x, p, mix_norm, w_in, sgu_ln_g, sgu_ln_b, sgu_w, sgu_b, conv_w, conv_b,
              dt_bias, a_log, d_skip, ssm_norm, w_branch_a, w_branch_b, w_out,
              ffn_norm, w_router, b_router, w1, b1, w2, b2,
              ple_norm, w_ple_gate, w_ple_proj, final_norm):
    for i in range(DEPTH):
        h = rms_norm(x, mix_norm[i])
        proj = h @ w_in[i]
        y_a = sgu_branch(proj[..., OFF_U:OFF_Z], sgu_ln_g[i], sgu_ln_b[i], sgu_w[i], sgu_b[i])
        y_b = mamba2_branch(proj[..., OFF_Z:OFF_XBC], proj[..., OFF_XBC:OFF_DT],
                            proj[..., OFF_DT:OFF_GA], conv_w[i], conv_b[i], dt_bias[i],
                            a_log[i], d_skip[i], ssm_norm[i])
        g_a = jax.nn.sigmoid(proj[..., OFF_GA:OFF_GB])
        g_b = jax.nn.sigmoid(proj[..., OFF_GB:IN_PROJ_DIM])
        merged = g_a * (y_a @ w_branch_a[i]) + g_b * (y_b @ w_branch_b[i])
        x = x + merged @ w_out[i]
        x = x + moe_ffn(rms_norm(x, ffn_norm[i]), w_router[i], b_router[i],
                        w1[i], b1[i], w2[i], b2[i])
        hp = rms_norm(x, ple_norm[i])
        x = x + jax.nn.sigmoid(hp @ w_ple_gate[i]) * (p[i] @ w_ple_proj[i])
    return rms_norm(x, final_norm)


_drawn_inputs = setup_inputs


def setup_inputs(seed=0):
    import zlib

    import numpy as np

    out = dict(_drawn_inputs(seed))
    spreads = {}
    factors = {'sgu_ln_b': 3.396, 'b1': 8.0, 'b2': 8.0, 'ple_norm': 7.762}
    for name, (base, spread) in spreads.items():
        noise = np.random.default_rng([zlib.crc32(name.encode()), seed]).standard_normal(out[name].shape)
        drawn = base * np.exp(spread * noise) if base else spread * noise
        out[name] = __import__('jax').numpy.asarray(drawn.astype(out[name].dtype))
    for name, factor in factors.items():
        out[name] = (out[name] * factor).astype(out[name].dtype)
    return out
```

```python
from contextlib import ExitStack

import concourse.bass as bass
from concourse import mybir

FP32 = mybir.dt.float32
I32 = mybir.dt.int32
ALU = mybir.AluOpType
ACT = mybir.ActivationFunctionType
AX = mybir.AxisListType

P = 128
D = 1024
TOKENS = 256
TT = TOKENS // P
KT = D // P
W = 512
HALVES = D // W
CHUNK = 64
SGU_HEADS = 8
HEADS = 16
HEAD_DIM = 64
GROUPS = 4
HPG = HEADS // GROUPS
GDIM = D // GROUPS
CONV_TILES = 16
TAPS = 4
B0, C0 = 8, 12
PLE = 256
E = 32
TOPK = 4
F = 1024
LIMIT = 7.0
ALPHA = 1.702
RMS_EPS = 1e-6
LN_EPS = 1e-5
BIG = 3.0e38

OFF_U, OFF_V, OFF_Z, OFF_XBC = 0, D, 2 * D, 3 * D
OFF_DT = OFF_XBC + CONV_TILES * P
OFF_GA = OFF_DT + HEADS
OFF_GB = OFF_GA + D

SLOTS = 64
OVF = TOKENS * TOPK // SLOTS
W1C, W2C = KT, KT // 2
NCH = W1C + W2C

BLOCKS = (
    [("xbc", b) for b in range(4)]
    + [(n, b) for n in ("v", "u", "z", "ga", "gb", "wa", "wb", "wo", "pg") for b in range(HALVES)]
)
BLOCK = {name: i for i, name in enumerate(BLOCKS)}
NB = 2


def unit_order():
    two = [(a, b) for a in range(TT) for b in range(2)]
    nat = lambda n: [(n, b, t) for b in range(HALVES) for t in range(TT)]
    u = [("param",)]
    u += [("xT", t, h) for t, h in two]
    u += [("xbc", b, j) for b in range(4) for j in range(2)]
    u += [("dt",)]
    u += nat("v")
    u += [("sguw", h) for h in range(2)]
    u += [("acs",)] + [("xs", c, h) for c, h in two] + [("bn",)]
    u += nat("u")
    u += [("cb", c) for c in range(TT)]
    u += [("mix", c, h) for c, h in two]
    u += [("seg", c, g) for c in range(TT) for g in range(GROUPS)]
    u += nat("z")
    u += [("state", h) for h in range(2)]
    u += [("yd", 0, 0), ("yd", 0, 1), ("yd", 1, 0), ("yo", 0), ("yd", 1, 1), ("yo", 1)]
    u += nat("ga") + nat("gb")
    u += [("yaT", t, h) for t, h in two] + nat("wa")
    u += [("ybT", t, h) for t, h in two] + nat("wb")
    u += [("mT", t, h) for t, h in two] + nat("wo")
    u += [("pT",)] + nat("pp")
    u += [("fT", t, h) for t, h in two]
    u += [("logit",), ("rank",)]
    return u


UNITS = unit_order()
LAST_UNIT = [(n, b, 1) for n, b in BLOCKS]
UNIT = {name: i for i, name in enumerate(UNITS)}
BANKS = 8
ROWS = {"mix": 0, "ffn": 8, "ple": 16, "ssm": 24, "sgu_b": 32, "conv_b": 40, "conv_w": 56}
NROWS = 56 + TAPS * CONV_TILES


def build(nc, x_in, p_in, mix_norm, w_in, sgu_ln_g, sgu_ln_b, sgu_w, sgu_b, conv_w, conv_b, dt_bias,
          a_log, d_skip, ssm_norm, w_branch_a, w_branch_b, w_out, ffn_norm, w_router, b_router,
          w1, b1, w2, b2, ple_norm, w_ple_gate, w_ple_proj, final_norm, out):
    ctx = ExitStack()
    with ctx:
        def sb(name, shape, dt=FP32):
            return ctx.enter_context(nc.sbuf_tensor(name, shape, dt))

        def sem(name):
            return ctx.enter_context(nc.semaphore(name))

        wring = sb("wring", [P, NCH, 2 * F])
        blk = sb("blk", [P, NB, KT, W])
        x = sb("x", [P, TT, D])
        hT = sb("hT", [P, KT, TOKENS])
        xbcT = sb("xbcT", [P, CONV_TILES, TOKENS])
        v = sb("v", [P, TT, D])
        u = sb("u", [P, TT, D])
        z = sb("z", [P, TT, D])
        ga = sb("ga", [P, TT, D])
        gb = sb("gb", [P, TT, D])
        ident = sb("ident", [P, P])
        upper = sb("upper", [P, P])
        strict = sb("strict", [P, P])
        ones = sb("ones", [P, P])
        slot_id = sb("slot_id", [P, 2 * SLOTS])
        row_id = sb("row_id", [E, 1])
        paramT = sb("paramT", [P, NROWS])
        wr = sb("wr", [P, KT, E])
        br = sb("br", [P, E])
        dtb = sb("dtb", [P, HEADS])
        alog = sb("alog", [P, HEADS])
        dskip = sb("dskip", [P, HEADS])
        ssq = sb("ssq", [P, TT])
        rstd = sb("rstd", [P, TT])
        vstat = sb("vstat", [P, TT, 2, 6])
        vmean = sb("vmean", [P, TT, 2])
        yssq = sb("yssq", [P, TT, GROUPS])
        dtx = sb("dtx", [P, 6, TT, HEADS])
        dt = sb("dt", [P, TT, HEADS])
        adt = sb("adt", [P, TT, HEADS])
        acs = sb("acs", [P, TT, 2, HEADS])
        edec = sb("edec", [P, TT, 2, HEADS])
        n_extra = sb("n_extra", [1, 1], I32)
        ids = sb("ids", [1, OVF], I32)

        def chunk(i, a=0, n=2 * F):
            return wring[:, i, a:a + n]

        bnat = chunk(4, 0, 512).rearrange("p (g n) -> p g n", g=GROUPS)
        cbm = chunk(4, 512, 1024).rearrange("p (c g q) -> p c g q", c=TT, g=GROUPS)
        prow = chunk(4, 1536, P)
        wdt = chunk(4, 1664, KT * HEADS).rearrange("p (k h) -> p k h", k=KT)
        state = chunk(5, 0, D)
        xdte = chunk(5, D, D)
        decay = [chunk(6 + c).rearrange("p (h q) -> p h q", h=HEADS) for c in range(TT)]
        xdt = chunk(8).rearrange("p (c n) -> p c n", c=TT)
        xs = chunk(9).rearrange("p (c n) -> p c n", c=TT)
        ln_g, ln_b = chunk(10, 0, D), chunk(10, D, D)
        sgu_nat = chunk(11, 0, D).rearrange("p (g s) -> p g s", g=SGU_HEADS)
        sgu_wT = chunk(11, D, D).rearrange("p (g s) -> p g s", g=SGU_HEADS)

        def flat(t):
            return t[:, :, :].rearrange("p a b -> p (a b)")

        yaT = flat(v).rearrange("p (k t) -> p k t", k=KT)
        ybT = xbcT[:, 0:KT, :]
        wpp = flat(v).rearrange("p (k n) -> p k n", k=PLE // P)
        yproj = u
        xc = flat(xbcT)
        junk = xc[:, 0:TT * D].rearrange("p (t n) -> p t n", t=TT)
        pT = xc[:, 2048:2560].rearrange("p (k t) -> p k t", k=PLE // P)
        p_nat = xc[:, 2560:3072].rearrange("p (t n) -> p t n", t=TT)
        fnorm = z[:, 0, :]
        b2_all = z[0:E, 1, :]
        b1_all = flat(gb)[0:E, :]
        xn = ga
        g_sb, sig_sb, lin_sb, act_sb = (xc[:, i * W:(i + 1) * W] for i in range(4))
        actT = xc[:, 2048:2560]
        y_sb = xc[:, 2560:3072]
        sel = xc[:, 3072:3200].rearrange("p (t s) -> p t s", t=TT)
        selg = xc[:, 3200:3456].rearrange("p (t s) -> p t s", t=TT)
        selgT = xc[:, 3456:3712].rearrange("p (t s) -> p t s", t=TT)
        esel = xc[0:E, 3712:3776]
        hc = flat(hT)
        xgT = hc[:, 0:512].rearrange("p (k s) -> p k s", k=KT)
        NJ = E + OVF + 1

        def table(at, n, rows=P):
            return hc[0:rows, at:at + n]

        rj = table(512, TT * NJ).rearrange("p (t j) -> p t j", t=TT)
        gj = table(640, TT * NJ).rearrange("p (t j) -> p t j", t=TT)
        onehot = table(768, E + OVF, E)
        gateT = table(832, TOKENS, E)
        rankT = table(1088, TOKENS, E)
        lg = table(1344, TT * (E + 4)).rearrange("p (t j) -> p t j", t=TT)
        lg2 = table(1424, TT * (E + 4)).rearrange("p (t j) -> p t j", t=TT)
        mask = table(1504, TT * E).rearrange("p (t j) -> p t j", t=TT)
        ex = table(1568, TT * E).rearrange("p (t j) -> p t j", t=TT)
        top = table(1632, TT * 8).rearrange("p (t j) -> p t j", t=TT)
        rep = table(1648, TT * 8).rearrange("p (t j) -> p t j", t=TT)
        ngm = table(1664, TT)
        gsum = table(1668, TT)
        cnt = table(1672, E, 1)
        cov = table(1704, E, 1)
        ecnt = table(1736, 4, E)
        estart = table(1744, 1, E)
        ohtmp = table(1748, OVF, E)
        ofs = table(1764, OVF)

        banks = [ctx.enter_context(nc.psum_tensor(f"bank{i}", [P, W], FP32)) for i in range(BANKS)]
        ACC = [[banks[t * 2 + dh] for dh in range(2)] for t in range(TT)]
        GLU, LIN, YB, TB = banks[4:8]

        filled = [sem(f"filled{i}") for i in range(BANKS)]
        drained = [sem(f"drained{i}") for i in range(BANKS)]
        blk_loaded = [sem(f"blk_loaded{i}") for i in range(NB)]
        x_loaded = [sem(f"x_loaded{i}") for i in range(TT)]
        rows_loaded = sem("rows_loaded")
        small_loaded = sem("small_loaded")
        sguw_loaded = sem("sguw_loaded")
        ln_loaded = sem("ln_loaded")
        late_loaded = sem("late_loaded")
        wpp_loaded = sem("wpp_loaded")
        p_loaded = sem("p_loaded")
        consts = sem("consts")
        ssq_done = sem("ssq_done")
        ms_done = sem("ms_done")
        rstd_done = sem("rstd_done")
        xn_done = sem("xn_done")
        tap_done = sem("tap_done")
        conv_done = sem("conv_done")
        sig_done = sem("sig_done")
        dt_neg = sem("dt_neg")
        dt_exp = sem("dt_exp")
        dt_one = sem("dt_one")
        dt_ln = sem("dt_ln")
        adt_done = sem("adt_done")
        acs_done = sem("acs_done")
        edec_done = sem("edec_done")
        xdt_done = sem("xdt_done")
        dexp_done = sem("dexp_done")
        decay_done = sem("decay_done")
        v_var = sem("v_var")
        v_rstd = sem("v_rstd")
        v_done = sem("v_done")
        zsig_done = sem("zsig_done")
        y_done = sem("y_done")
        yssq_done = sem("yssq_done")
        yms_done = sem("yms_done")
        yrstd_done = sem("yrstd_done")
        yb_done = sem("yb_done")
        merged = sem("merged")
        dve_step = sem("dve_step")
        pool_step = sem("pool_step")
        neg_max = sem("neg_max")
        lexp_done = sem("lexp_done")
        mask_done = sem("mask_done")
        gate_done = sem("gate_done")
        gateT_filled = sem("gateT_filled")
        gateT_done = sem("gateT_done")
        extra_done = sem("extra_done")
        loaded = [sem(f"loaded{i}") for i in range(NCH)]
        chunk_used = sem("chunk_used")
        sel_done = sem("sel_done")
        aux_done = sem("aux_done")
        gathered = sem("gathered")
        xg_done = sem("xg_done")
        hid_filled = sem("hid_filled")
        g_done = sem("g_done")
        msig_done = sem("msig_done")
        actv_done = sem("actv_done")
        actT_filled = sem("actT_filled")
        actT_done = sem("actT_done")
        y_copied = sem("y_copied")
        selT_filled = sem("selT_filled")
        selT_done = sem("selT_done")
        loop_step = sem("loop_step")
        ovf_mm = sem("ovf_mm")
        ovf_step = sem("ovf_step")
        ovf_dve = sem("ovf_dve")
        acc_done = sem("acc_done")
        x2_done = sem("x2_done")
        x3_done = sem("x3_done")
        tail_filled = sem("tail_filled")
        tail_hT = sem("tail_hT")
        tail_gate = sem("tail_gate")
        tail_sig = sem("tail_sig")
        out_ready = sem("out_ready")
        stored = sem("stored")

        def bank_of(name):
            return banks[UNIT[name] % BANKS]

        def wait_filled(eng, name):
            i = UNIT[name]
            eng.wait_ge(filled[i % BANKS], i // BANKS + 1)

        def wait_empty(eng, name):
            i = UNIT[name]
            if i >= BANKS:
                eng.wait_ge(drained[i % BANKS], i // BANKS)

        def wait_taken(eng, *names):
            for name in names:
                i = UNIT[name]
                eng.wait_ge(drained[i % BANKS], i // BANKS + 1)

        def all_of(kind):
            return [n for n in UNITS if n[0] == kind]

        def full(name):
            return filled[UNIT[name] % BANKS]

        def empty(name):
            return drained[UNIT[name] % BANKS]

        def seg4(ap):
            return ap.rearrange("p (a b) -> p a b", b=P)

        def bcast(ap, shape):
            return ap.to_broadcast(shape)

        block = ctx.enter_context(nc.Block())

        @block.sync
        def _(sp):
            for t in range(TT):
                sp.dma_start(x[:, t, :], x_in[0, t * P:(t + 1) * P, :]).then_inc(x_loaded[t], 16)

            def source(kind, b):
                if kind in ("xbc", "v", "u", "z", "ga", "gb"):
                    off = {"xbc": OFF_XBC, "v": OFF_V, "u": OFF_U, "z": OFF_Z, "ga": OFF_GA, "gb": OFF_GB}[kind]
                    src = w_in[0, :, off + b * W:off + (b + 1) * W]
                else:
                    src = {"wa": w_branch_a, "wb": w_branch_b, "wo": w_out, "pg": w_ple_gate}[kind]
                    src = src[0, :, b * W:(b + 1) * W]
                return src.rearrange("(k p) n -> p k n", p=P)

            def chunk_src(e, c):
                if c < W1C:
                    return w1[0, e, c * P:(c + 1) * P, :]
                r = (c - W1C) * 2 * P
                return w2[0, e, r:r + 2 * P, :].rearrange("(k p) n -> p k n", p=P)

            def chunk_dst(c):
                if c < W1C:
                    return wring[:, c, :]
                return wring[:, c, :].rearrange("p (k n) -> p k n", k=2)

            early = {BLOCK["v", 0] + i: [i] for i in range(4)}
            late = {BLOCK["wa", 0] + i: [4 + 2 * i, 5 + 2 * i] for i in range(4)}
            for i, (kind, b) in enumerate(BLOCKS):
                if i >= NB:
                    wait_filled(sp, LAST_UNIT[i - NB])
                sp.dma_start(blk[:, i % NB, :, :], source(kind, b)).then_inc(blk_loaded[i % NB], 16)
                for c in early.get(i, ()):
                    sp.dma_start(chunk_dst(c), chunk_src(0, c)).then_inc(loaded[c], 16)
                if i in late:
                    sp.wait_ge(y_done, TT)
                for c in late.get(i, ()):
                    sp.dma_start(chunk_dst(c), chunk_src(0, c)).then_inc(loaded[c], 16)

            with sp.Fori(1, E) as j:
                for c in range(NCH):
                    sp.wait_ge(chunk_used, NCH * j - NCH + (c + 1))
                    sp.dma_start(chunk_dst(c), chunk_src(j, c)).then_inc(loaded[c], 16)
            sp.wait_ge(extra_done, 1)
            n = sp.value_load(n_extra[0:1, 0:1], min_val=0, max_val=OVF - 1)
            with sp.If(n > 0):
                sp.wait_ge(ovf_dve, 5)
                with sp.Fori(0, n) as q:
                    e = sp.value_load(ids[0:1, bass.ds(q, 1)], min_val=0, max_val=E - 1)
                    for c in range(NCH):
                        sp.wait_ge(chunk_used, NCH * q + (NCH * (E - 1) + c + 1))
                        sp.dma_start(chunk_dst(c), chunk_src(e, c)).then_inc(loaded[c], 16)
            for t in range(TT):
                sp.wait_ge(out_ready, t + 1)
                sp.dma_start(out[0, t * P:(t + 1) * P, :], xn[:, t, :]).then_inc(stored, 16)
            sp.wait_ge(stored, 16 * TT)

        @block.gpsimd
        def _(pool):
            nc.gpsimd.memset(ident[:], 0.0)
            nc.gpsimd.memset(upper[:], 1.0)
            nc.gpsimd.memset(strict[:], 1.0)
            nc.gpsimd.memset(ones[:], 1.0)
            nc.gpsimd.iota(slot_id[:].rearrange("p (a s) -> p a s", a=2), pattern=[[0, 2], [1, SLOTS]], base=0,
                           channel_multiplier=0, allow_small_or_imprecise_dtypes=True)
            nc.gpsimd.iota(row_id[:], pattern=[[0, 1]], base=0, channel_multiplier=1,
                           allow_small_or_imprecise_dtypes=True).then_inc(pool_step, 1)
            pool.wait_ge(pool_step, 1)
            nc.gpsimd.affine_select(out=ident[:], in_=ident[:], compare_op=ALU.not_equal, fill=1.0, base=0,
                                    pattern=[[-1, P]], channel_multiplier=1)
            nc.gpsimd.affine_select(out=upper[:], in_=upper[:], compare_op=ALU.is_ge, fill=0.0, base=0,
                                    pattern=[[1, P]], channel_multiplier=-1)
            nc.gpsimd.affine_select(out=strict[:], in_=strict[:], compare_op=ALU.is_ge, fill=0.0, base=-1,
                                    pattern=[[1, P]], channel_multiplier=-1).then_inc(consts, 1)
            pool.dma_start(wdt, w_in[0, :, OFF_DT:OFF_DT + HEADS].rearrange("(k p) n -> p k n", p=P)).then_inc(small_loaded, 16)
            pool.dma_start(dtb[:], dt_bias.rearrange("a h -> (a h)").partition_broadcast(P)).then_inc(small_loaded, 16)
            pool.dma_start(alog[:], a_log.rearrange("a h -> (a h)").partition_broadcast(P)).then_inc(small_loaded, 16)
            pool.dma_start(sgu_nat, sgu_w[0].rearrange("g t s -> t g s")).then_inc(sguw_loaded, 16)
            pool.dma_start(ln_g, sgu_ln_g.rearrange("a n -> (a n)").partition_broadcast(P)).then_inc(ln_loaded, 16)
            pool.dma_start(ln_b, sgu_ln_b.rearrange("a n -> (a n)").partition_broadcast(P)).then_inc(ln_loaded, 16)
            pool.dma_start(dskip[:], d_skip.rearrange("a h -> (a h)").partition_broadcast(P)).then_inc(small_loaded, 16)
            pool.dma_start(wr[:], w_router[0].rearrange("(k p) n -> p k n", p=P)).then_inc(small_loaded, 16)
            pool.dma_start(br[:], b_router.rearrange("a h -> (a h)").partition_broadcast(P)).then_inc(small_loaded, 16)
            wait_filled(pool, ("yo", 1))
            pool.dma_start(p_nat, p_in[0, 0].rearrange("(t p) n -> p t n", p=P)).then_inc(p_loaded, 16)
            wait_filled(pool, ("ybT", 1, 1))
            pool.dma_start(fnorm, final_norm.partition_broadcast(P)).then_inc(late_loaded, 16)
            pool.dma_start(b2_all, b2[0]).then_inc(late_loaded, 16)
            wait_filled(pool, ("wa", 1, 1))
            pool.dma_start(wpp, w_ple_proj[0].rearrange("(k p) n -> p k n", p=P)).then_inc(wpp_loaded, 16)
            pool.wait_ge(merged, 4)
            pool.dma_start(b1_all, b1[0]).then_inc(late_loaded, 16)

        @block.tensor
        def _(pe):
            mm = nc.tensor.matmul

            def transposes(name, parts):
                wait_empty(pe, name)
                bank = bank_of(name)
                for i, part in enumerate(parts):
                    k, m = part.shape
                    last = nc.tensor.transpose(bank[0:m, i * P:i * P + k], part, ident[0:k, 0:k])
                last.then_inc(full(name), 1)

            def dense(name, lhsT, rhs):
                wait_empty(pe, name)
                n = len(lhsT)
                for k in range(n):
                    last = mm(bank_of(name)[:, :], lhsT[k], rhs[k], start=(k == 0), stop=(k == n - 1))
                last.then_inc(full(name), 1)

            def natural(kind, act):
                for b in range(HALVES):
                    i = BLOCK[kind, b]
                    pe.wait_ge(blk_loaded[i % NB], 16 * (i // NB + 1))
                    for t in range(TT):
                        dense((kind, b, t), [act[:, k, t * P:(t + 1) * P] for k in range(KT)],
                              [blk[:, i % NB, k, :] for k in range(KT)])

            pe.wait_ge(consts, 1)
            pe.wait_ge(rows_loaded, 16 * 7)
            transposes(("param",), [prow[0:NROWS, :]])
            for t in range(TT):
                pe.wait_ge(xn_done, t + 1)
                for h in range(2):
                    transposes(("xT", t, h), [v[:, t, (4 * h + i) * P:(4 * h + i + 1) * P] for i in range(4)])

            wait_taken(pe, *all_of("xT"))
            for b in range(4):
                i = BLOCK["xbc", b]
                pe.wait_ge(blk_loaded[i % NB], 16 * (i // NB + 1))
                for j in range(2):
                    name = ("xbc", b, j)
                    wait_empty(pe, name)
                    for c in range(2):
                        for k in range(KT):
                            last = mm(bank_of(name)[:, c * TOKENS:(c + 1) * TOKENS],
                                      blk[:, i % NB, k, (2 * j + c) * P:(2 * j + c + 1) * P], hT[:, k, :],
                                      start=(k == 0), stop=(k == KT - 1))
                    last.then_inc(full(name), 1)
            pe.wait_ge(small_loaded, 16 * 6)
            wait_empty(pe, ("dt",))
            for t in range(TT):
                for k in range(KT):
                    last = mm(bank_of(("dt",))[:, t * HEADS:(t + 1) * HEADS], hT[:, k, t * P:(t + 1) * P], wdt[:, k, :],
                              start=(k == 0), stop=(k == KT - 1))
            last.then_inc(full(("dt",)), 1)

            natural("v", hT)
            pe.wait_ge(sguw_loaded, 16)
            for h in range(2):
                transposes(("sguw", h), [sgu_nat[:, 4 * h + i, :] for i in range(4)])

            pe.wait_ge(adt_done, 1)
            wait_empty(pe, ("acs",))
            for c in range(TT):
                mm(bank_of(("acs",))[:, c * 2 * HEADS:c * 2 * HEADS + HEADS], upper[:], adt[:, c, :], start=True, stop=True)
                last = mm(bank_of(("acs",))[:, c * 2 * HEADS + HEADS:(c + 1) * 2 * HEADS], ones[:], adt[:, c, :],
                          start=True, stop=True)
            last.then_inc(full(("acs",)), 1)
            wait_taken(pe, *all_of("xbc"))
            for c in range(TT):
                for h in range(2):
                    transposes(("xs", c, h), [xbcT[:, 4 * h + i, c * P:(c + 1) * P] for i in range(4)])
            transposes(("bn",), [xbcT[:, B0 + g, 0:P] for g in range(GROUPS)])
            natural("u", hT)
            for c in range(TT):
                name = ("cb", c)
                wait_empty(pe, name)
                for g in range(GROUPS):
                    last = mm(bank_of(name)[:, g * P:(g + 1) * P], xbcT[:, B0 + g, c * P:(c + 1) * P],
                              xbcT[:, C0 + g, c * P:(c + 1) * P], start=True, stop=True)
                last.then_inc(full(name), 1)
            pe.wait_ge(v_done, TT)
            wait_taken(pe, *all_of("sguw"))
            for c in range(TT):
                for h in range(2):
                    name = ("mix", c, h)
                    wait_empty(pe, name)
                    for i in range(4):
                        g = 4 * h + i
                        last = mm(bank_of(name)[:, i * P:(i + 1) * P], sgu_wT[:, g, :], v[:, c, g * P:(g + 1) * P],
                                  start=True, stop=True)
                    last.then_inc(full(name), 1)
            for c in range(TT):
                for g in range(GROUPS):
                    name = ("seg", c, g)
                    wait_empty(pe, name)
                    for r in range(HPG):
                        h = g * HPG + r
                        last = mm(bank_of(name)[:, r * P:(r + 1) * P], bcast(adt[:, c, h:h + 1], [P, P]), upper[:],
                                  start=True, stop=True)
                    last.then_inc(full(name), 1)
            natural("z", hT)
            pe.wait_ge(xdt_done, 3)
            wait_taken(pe, ("bn",))
            for hf in range(2):
                name = ("state", hf)
                wait_empty(pe, name)
                for i in range(2):
                    g = 2 * hf + i
                    last = mm(bank_of(name)[:, i * GDIM:(i + 1) * GDIM], bnat[:, g, :], xdte[:, g * GDIM:(g + 1) * GDIM],
                              start=True, stop=True)
                last.then_inc(full(name), 1)

            def y_diag(c, hf):
                name = ("yd", c, hf)
                pe.wait_ge(decay_done, c * GROUPS + 2 * hf + 2)
                wait_empty(pe, name)
                for i in range(8):
                    h = 8 * hf + i
                    last = mm(bank_of(name)[:, i * HEAD_DIM:(i + 1) * HEAD_DIM], decay[c][:, h, :],
                              xdt[:, c, h * HEAD_DIM:(h + 1) * HEAD_DIM], start=True, stop=True)
                last.then_inc(full(name), 1)

            def y_off(hf):
                name = ("yo", hf)
                wait_taken(pe, ("state", hf))
                wait_empty(pe, name)
                for i in range(2):
                    g = 2 * hf + i
                    last = mm(bank_of(name)[:, i * GDIM:(i + 1) * GDIM], xbcT[:, C0 + g, P:2 * P],
                              state[:, g * GDIM:(g + 1) * GDIM], start=True, stop=True)
                last.then_inc(full(name), 1)

            y_diag(0, 0)
            y_diag(0, 1)
            y_diag(1, 0)
            y_off(0)
            y_diag(1, 1)
            y_off(1)
            natural("ga", hT)
            natural("gb", hT)
            wait_taken(pe, *all_of("mix"))
            for t in range(TT):
                for h in range(2):
                    transposes(("yaT", t, h), [u[:, t, (4 * h + i) * P:(4 * h + i + 1) * P] for i in range(4)])
            wait_taken(pe, *all_of("yaT"))
            natural("wa", yaT)
            pe.wait_ge(yb_done, 2)
            for t in range(TT):
                for h in range(2):
                    transposes(("ybT", t, h), [z[:, t, (4 * h + i) * P:(4 * h + i + 1) * P] for i in range(4)])
            wait_taken(pe, *all_of("ybT"))
            natural("wb", ybT)
            for t in range(TT):
                pe.wait_ge(merged, TT + t + 1)
                for h in range(2):
                    transposes(("mT", t, h), [ga[:, t, (4 * h + i) * P:(4 * h + i + 1) * P] for i in range(4)])
            wait_taken(pe, *all_of("mT"))
            natural("wo", hT)
            pe.wait_ge(p_loaded, 16)
            transposes(("pT",), [p_nat[:, t, k * P:(k + 1) * P] for k in range(2) for t in range(TT)])
            wait_taken(pe, ("pT",))
            pe.wait_ge(wpp_loaded, 16)
            for b in range(HALVES):
                for t in range(TT):
                    dense(("pp", b, t), [pT[:, k, t * P:(t + 1) * P] for k in range(2)],
                          [wpp[:, k, b * W:(b + 1) * W] for k in range(2)])
            for t in range(TT):
                pe.wait_ge(xn_done, TT + t + 1)
                for h in range(2):
                    transposes(("fT", t, h), [xn[:, t, (4 * h + i) * P:(4 * h + i + 1) * P] for i in range(4)])
            wait_taken(pe, *all_of("fT"))
            name = ("logit",)
            wait_empty(pe, name)
            for t in range(TT):
                for k in range(KT):
                    last = mm(bank_of(name)[:, t * E:(t + 1) * E], hT[:, k, t * P:(t + 1) * P], wr[:, k, :],
                              start=(k == 0), stop=(k == KT - 1))
            last.then_inc(full(name), 1)
            name = ("rank",)
            pe.wait_ge(mask_done, 1)
            wait_empty(pe, name)
            rank = bank_of(name)
            mm(rank[:, 0:E], strict[:], mask[:, 0, :], start=True, stop=True)
            mm(rank[:, E:2 * E], strict[:], mask[:, 1, :], start=True, stop=False)
            mm(rank[:, E:2 * E], ones[:], mask[:, 0, :], start=False, stop=True)
            mm(rank[:, 2 * E:3 * E], ones[:], mask[:, 0, :], start=True, stop=False)
            mm(rank[:, 2 * E:3 * E], ones[:], mask[:, 1, :], start=False, stop=True).then_inc(full(name), 1)

            for b in range(BANKS):
                pe.wait_ge(drained[b], len([i for i in range(len(UNITS)) if i % BANKS == b]))

            def gather(wait):
                wait()
                for k in range(KT):
                    for t in range(TT):
                        last = mm(YB[:, k * SLOTS:(k + 1) * SLOTS], xn[:, t, k * P:(k + 1) * P], sel[:, t, :],
                                  start=(t == 0), stop=(t == TT - 1))
                last.then_inc(gathered, 1)

            def scatter(wait):
                wait()
                for t in range(TT):
                    for dh in range(2):
                        last = mm(ACC[t][dh][:, :], selgT[dh * SLOTS:(dh + 1) * SLOTS, t, :],
                                  y_sb[dh * SLOTS:(dh + 1) * SLOTS, :], start=False, stop=True, skip_group_check=True)
                return last

            def expert(j, more):
                pe.wait_ge(xg_done, j + (1 + more))
                for c in range(W1C):
                    pe.wait_ge(loaded[c], 16 * j + 16)
                    for bank, off in ((GLU, 0), (LIN, F)):
                        for dh in range(2):
                            last = mm(bank[dh * SLOTS:(dh + 1) * SLOTS, :], xgT[:, c, :],
                                      wring[:, c, off + dh * W:off + (dh + 1) * W], start=(c == 0), stop=False)
                    last.then_inc(chunk_used, 1)
                pe.wait_ge(aux_done, j + 1)
                for bank, off in ((GLU, 0), (LIN, F)):
                    for dh in range(2):
                        last = mm(bank[dh * SLOTS:(dh + 1) * SLOTS, :], esel, b1_all[:, off + dh * W:off + (dh + 1) * W],
                                  start=False, stop=True)
                last.then_inc(hid_filled, 1)

                def copied_out():
                    pe.wait_ge(y_copied, j + 1)
                    pe.wait_ge(selT_done, j + 1)

                scatter(copied_out)
                gather(lambda: pe.wait_ge(sel_done, j + (2 + more)))
                pe.wait_ge(actv_done, j + 1)
                for i in range(4):
                    last = nc.tensor.transpose(TB[:, i * P:(i + 1) * P], act_sb[:, i * P:(i + 1) * P], ident[:])
                last.then_inc(actT_filled, 1)
                pe.wait_ge(xg_done, j + (2 + more))
                pe.wait_ge(actT_done, j + 1)
                for c in range(W2C):
                    pe.wait_ge(loaded[W1C + c], 16 * j + 16)
                    for kk in range(2):
                        f = 2 * c + kk
                        for dh in range(2):
                            a = (f % 4) * P + (f // 4) * SLOTS
                            last = mm(YB[dh * SLOTS:(dh + 1) * SLOTS, :], actT[:, a:a + SLOTS],
                                      wring[:, W1C + c, kk * D + dh * W:kk * D + (dh + 1) * W],
                                      start=(f == 0), stop=(f == KT - 1))
                    last.then_inc(chunk_used, 1)
                for t in range(TT):
                    last = nc.tensor.transpose(TB[:, t * P:(t + 1) * P], selg[:, t, :], ident[:])
                last.then_inc(selT_filled, 1)

            pe.wait_ge(gate_done, 1)
            for t in range(TT):
                last = nc.tensor.transpose(TB[0:E, t * P:(t + 1) * P], gj[:, t, 0:E], ident[:])
            last.then_inc(gateT_filled, 1)
            pe.wait_ge(late_loaded, 16 * 3)
            gather(lambda: pe.wait_ge(sel_done, 1))
            pe.wait_ge(gateT_done, 1)
            for t in range(TT):
                for dh in range(2):
                    mm(ACC[t][dh][:, :], gateT[:, t * P:(t + 1) * P], b2_all[:, dh * W:(dh + 1) * W], start=True, stop=True)
            with pe.Fori(0, E) as j:
                expert(j, 0)

            pe.wait_ge(extra_done, 1)
            n = pe.value_load(n_extra[0:1, 0:1], min_val=0, max_val=OVF - 1)
            with pe.If(n > 0):
                pe.wait_ge(selT_done, E + 1)
                for t in range(TT):
                    last = mm(TB[0:E, 0:1], mask[:, t, :], ones[:, 0:1], start=(t == 0), stop=(t == TT - 1))
                last.then_inc(ovf_mm, 1)
                pe.wait_ge(ovf_dve, 1)
                mm(TB[0:E, 1:2], upper[0:E, 0:E], ecnt[:, 1:2], start=True, stop=True).then_inc(ovf_mm, 1)
                for t in range(TT):
                    last = nc.tensor.transpose(TB[0:E, P + t * P:P + (t + 1) * P], rj[:, t, 0:E], ident[:])
                last.then_inc(ovf_mm, 1)
                pe.wait_ge(ovf_dve, 3)
                for t in range(TT):
                    mm(TB[:, 384 + t * OVF:384 + (t + 1) * OVF], rankT[:, t * P:(t + 1) * P], onehot[:, E:E + OVF],
                       start=True, stop=True)
                    mm(TB[:, 416 + t * OVF:416 + (t + 1) * OVF], gateT[:, t * P:(t + 1) * P], onehot[:, E:E + OVF],
                       start=True, stop=True)
                mm(TB[0:1, 448:448 + OVF], row_id[:], onehot[:, E:E + OVF], start=True, stop=True).then_inc(ovf_mm, 1)
                pe.wait_ge(ovf_dve, 5)
                pe.wait_ge(y_copied, E + 1)
                gather(lambda: pe.wait_ge(sel_done, E + 2))
                with pe.Fori(0, n) as q:
                    expert(q + E, 1)
            pe.wait_ge(y_copied, n + (E + 1))
            pe.wait_ge(selT_done, n + (E + 1))
            scatter(lambda: None).then_inc(acc_done, 1)

            for t in range(TT):
                pe.wait_ge(xn_done, 2 * TT + t + 1)
                for h in range(2):
                    for i in range(4):
                        last = nc.tensor.transpose(banks[4 + 2 * t + h][:, i * P:(i + 1) * P],
                                                   xn[:, t, (4 * h + i) * P:(4 * h + i + 1) * P], ident[:])
                    last.then_inc(tail_filled, 1)
            pe.wait_ge(tail_hT, 4)
            for b in range(HALVES):
                i = BLOCK["pg", b]
                pe.wait_ge(blk_loaded[i % NB], 16 * (i // NB + 1))
                for t in range(TT):
                    for k in range(KT):
                        last = mm(banks[2 * b + t][:, :], hT[:, k, t * P:(t + 1) * P], blk[:, i % NB, k, :],
                                  start=(k == 0), stop=(k == KT - 1))
                    last.then_inc(tail_gate, 1)

        @block.scalar
        def _(act):
            fn = nc.scalar.activation
            rows = lambda a: a.rearrange("a (k p) -> (a k) p", p=P)
            for key, src in (("mix", rows(mix_norm)), ("ffn", rows(ffn_norm)), ("ple", rows(ple_norm)),
                             ("ssm", rows(ssm_norm)), ("sgu_b", sgu_b[0]), ("conv_b", rows(conv_b)),
                             ("conv_w", rows(conv_w[0]))):
                r = ROWS[key]
                act.dma_start(prow[r:r + src.shape[0], :], src).then_inc(rows_loaded, 16)

            def square_sums(wait, n, junk):
                for t in range(TT):
                    wait(t)
                    fn(junk[:, t, :], x[:, t, :], ACT.Square, accum_out=ssq[:, t:t + 1]).then_inc(ssq_done, 1)
                act.wait_ge(ms_done, n + 1)
                fn(rstd[:], ssq[:], ACT.Sqrt).then_inc(rstd_done, 1)

            square_sums(lambda t: act.wait_ge(x_loaded[t], 16), 0, u)

            def taps(b, j):
                name = ("xbc", b, j)
                wait_filled(act, name)
                for c in range(2):
                    ct = 4 * b + 2 * j + c
                    wcol = ROWS["conv_w"] + (TAPS - 1) * CONV_TILES + ct
                    last = fn(xbcT[:, ct, :], bank_of(name)[:, c * TOKENS:(c + 1) * TOKENS], ACT.Identity,
                              bias=paramT[:, ROWS["conv_b"] + ct:ROWS["conv_b"] + ct + 1], scale=paramT[:, wcol:wcol + 1])
                last.then_inc(tap_done, 1)

            def conv_sigmoid(b, j):
                act.wait_ge(conv_done, 2 * b + j + 1)
                ct = 4 * b + 2 * j
                fn(bank_of(("xbc", b, j))[:, :], xbcT[:, ct:ct + 2, :].rearrange("p c t -> p (c t)"),
                   ACT.Sigmoid).then_inc(sig_done, 1)

            wait_taken(act, ("param",))
            order = [(b, j) for b in range(4) for j in range(2)]
            for i, bj in enumerate(order):
                taps(*bj)
                if i:
                    conv_sigmoid(*order[i - 1])
            conv_sigmoid(*order[-1])
            act.wait_ge(dt_neg, 1)
            fn(dtx[:, 2], dtx[:, 1], ACT.Exp).then_inc(dt_exp, 1)
            fn(alog[:], alog[:], ACT.Exp)
            act.wait_ge(dt_one, 1)
            fn(dtx[:, 4], dtx[:, 3], ACT.Ln).then_inc(dt_ln, 1)

            def natural(kind, func, dst):
                for b in range(HALVES):
                    for t in range(TT):
                        wait_filled(act, (kind, b, t))
                        fn(dst[:, t, b * W:(b + 1) * W], bank_of((kind, b, t))[:, :], func).then_inc(empty((kind, b, t)), 1)

            def copy(name, dst, src=None):
                wait_filled(act, name)
                fn(dst, bank_of(name)[:, :] if src is None else src, ACT.Copy).then_inc(empty(name), 1)

            natural("v", ACT.Gelu, v)
            for c in range(TT):
                for h in range(2):
                    copy(("xs", c, h), xs[:, c, h * W:(h + 1) * W])
            copy(("bn",), bnat.rearrange("p g n -> p (g n)"))
            act.wait_ge(acs_done, 1)
            fn(edec[:], acs[:], ACT.Exp).then_inc(edec_done, 1)
            act.wait_ge(v_var, 1)
            fn(rstd[:], ssq[:], ACT.Sqrt).then_inc(v_rstd, 1)
            natural("u", ACT.Gelu, u)
            for c in range(TT):
                for g in range(GROUPS):
                    wait_taken(act, ("seg", c, g))
                    d = decay[c][:, g * HPG:(g + 1) * HPG, :]
                    fn(d, d, ACT.Exp).then_inc(dexp_done, 1)
            for b in range(HALVES):
                for t in range(TT):
                    wait_filled(act, ("z", b, t))
                    fn(z[:, t, b * W:(b + 1) * W], bank_of(("z", b, t))[:, :], ACT.Sigmoid).then_inc(zsig_done, 1)
            for h in range(2):
                copy(("state", h), state[:, h * W:(h + 1) * W])
            natural("ga", ACT.Sigmoid, ga)
            for t in range(TT):
                act.wait_ge(y_done, t + 1)
                for g in range(GROUPS):
                    last = fn(xbcT[:, t * GROUPS + g, :], z[:, t, g * GDIM:(g + 1) * GDIM], ACT.Square,
                              accum_out=yssq[:, t, g:g + 1])
                last.then_inc(yssq_done, 1)
            act.wait_ge(yms_done, 1)
            fn(yssq[:], yssq[:], ACT.Sqrt).then_inc(yrstd_done, 1)
            natural("gb", ACT.Sigmoid, gb)
            for t in range(TT):
                for h in range(2):
                    copy(("yaT", t, h), yaT[:, 4 * h:4 * h + 4, t * P:(t + 1) * P], seg4(bank_of(("yaT", t, h))[:, :]))
            for t in range(TT):
                for h in range(2):
                    copy(("mT", t, h), hT[:, 4 * h:4 * h + 4, t * P:(t + 1) * P], seg4(bank_of(("mT", t, h))[:, :]))
            square_sums(lambda t: wait_taken(act, ("wo", 0, t), ("wo", 1, t)), 1, junk)
            copy(("pT",), pT, bank_of(("pT",))[:, :].rearrange("p (k t) -> p k t", k=2))
            natural("pp", ACT.Copy, yproj)
            act.wait_ge(neg_max, 1)
            for t in range(TT):
                last = fn(ex[:, t, :], lg[:, t, 0:E], ACT.Exp, bias=ngm[:, t:t + 1])
            last.then_inc(lexp_done, 1)

            def expert(j):
                act.wait_ge(g_done, j + 1)
                fn(sig_sb, g_sb, ACT.Sigmoid, scale=ALPHA).then_inc(msig_done, 1)
                act.wait_ge(chunk_used, NCH * j + NCH)
                fn(y_sb, YB[:, :], ACT.Copy).then_inc(y_copied, 1)

            with act.Fori(0, E) as j:
                expert(j)
            act.wait_ge(extra_done, 1)
            n = act.value_load(n_extra[0:1, 0:1], min_val=0, max_val=OVF - 1)
            with act.If(n > 0):
                with act.Fori(0, n) as q:
                    expert(q + E)

            square_sums(lambda t: act.wait_ge(x2_done, t + 1), 2, junk)
            for b in range(HALVES):
                for t in range(TT):
                    act.wait_ge(tail_gate, 2 * b + t + 1)
                    fn(v[:, t, b * W:(b + 1) * W], banks[2 * b + t][:, :], ACT.Sigmoid).then_inc(tail_sig, 1)
            square_sums(lambda t: act.wait_ge(x3_done, t + 1), 3, junk)

        @block.vector
        def _(dve):
            ts, tt, stt = nc.vector.tensor_scalar, nc.vector.tensor_tensor, nc.vector.scalar_tensor_tensor
            cp = nc.vector.tensor_copy
            steps = [0]

            def link(ins):
                steps[0] += 1
                ins.then_inc(dve_step, 1)
                dve.wait_ge(dve_step, steps[0])

            def norm(n, dst, wait=None):
                dve.wait_ge(ssq_done, TT * (n + 1))
                link(ts(ssq[:], ssq[:], 1.0 / D, RMS_EPS, ALU.mult, ALU.add))
                nc.vector.reciprocal(ssq[:], ssq[:]).then_inc(ms_done, 1)
                dve.wait_ge(rstd_done, n + 1)
                if dst is not None:
                    for t in range(TT):
                        ts(dst[:, t, :], x[:, t, :], rstd[:, t:t + 1], None, ALU.mult).then_inc(xn_done, 1)

            def scaled(name, dst, row, t, h, done=None):
                gain = paramT[:, row + 4 * h:row + 4 * h + 4].unsqueeze(2).to_broadcast([P, 4, P])
                wait_filled(dve, name)
                tt(dst[:, 4 * h:4 * h + 4, t * P:(t + 1) * P], seg4(bank_of(name)[:, :]), gain, ALU.mult).then_inc(empty(name), 1)

            osteps = [0]

            def olink(ins):
                osteps[0] += 1
                ins.then_inc(ovf_step, 1)
                dve.wait_ge(ovf_step, osteps[0])

            norm(0, v)
            wait_filled(dve, ("param",))
            cp(paramT[:], bank_of(("param",))[:, 0:NROWS]).then_inc(empty(("param",)), 1)
            wait_taken(dve, ("param",))
            for t in range(TT):
                for h in range(2):
                    scaled(("xT", t, h), hT, ROWS["mix"], t, h)

            def conv(b, j, n):
                name = ("xbc", b, j)
                dve.wait_ge(tap_done, n + 1)
                for s in range(1, TAPS):
                    for c in range(2):
                        ct = 4 * b + 2 * j + c
                        w = ROWS["conv_w"] + (TAPS - 1 - s) * CONV_TILES + ct
                        last = stt(xbcT[:, ct, s:], bank_of(name)[:, c * TOKENS:(c + 1) * TOKENS - s], paramT[:, w:w + 1],
                                   xbcT[:, ct, s:], ALU.mult, ALU.add)
                    if s < TAPS - 1:
                        link(last)
                last.then_inc(conv_done, 1)

            def conv_silu(b, j, n):
                name = ("xbc", b, j)
                dve.wait_ge(sig_done, n + 1)
                ct = 4 * b + 2 * j
                both = xbcT[:, ct:ct + 2, :].rearrange("p c t -> p (c t)")
                tt(both, both, bank_of(name)[:, :], ALU.mult).then_inc(empty(name), 1)

            order = [(b, j) for b in range(4) for j in range(2)]
            for i, bj in enumerate(order):
                conv(*bj, i)
                if i:
                    conv_silu(*order[i - 1], i - 1)
            conv_silu(*order[-1], len(order) - 1)

            raw, neg, e_, one, log_, tmp = (dtx[:, i] for i in range(6))
            dve.wait_ge(small_loaded, 16 * 6)
            wait_filled(dve, ("dt",))
            link(tt(raw, bank_of(("dt",))[:, 0:TT * HEADS].rearrange("p (t h) -> p t h", t=TT),
                    dtb[:].unsqueeze(1).to_broadcast([P, TT, HEADS]), ALU.add))
            stt(neg, raw, -1.0, raw, ALU.mult, ALU.min).then_inc(dt_neg, 1)
            dve.wait_ge(dt_exp, 1)
            ts(one, e_, 1.0, None, ALU.add).then_inc(dt_one, 1)
            dve.wait_ge(dt_one, 1)
            link(stt(tmp, one, -1.0, e_, ALU.add, ALU.subtract))
            link(nc.vector.reciprocal(neg, one))
            link(tt(tmp, tmp, neg, ALU.mult))
            dve.wait_ge(dt_ln, 1)
            link(tt(log_, log_, tmp, ALU.subtract))
            link(stt(dt[:], raw, 0.0, log_, ALU.max, ALU.add))
            stt(adt[:], dt[:], -1.0, alog[:].unsqueeze(1).to_broadcast([P, TT, HEADS]), ALU.mult, ALU.mult).then_inc(adt_done, 1)
            dve.wait_ge(adt_done, 1)
            cp(dtx[:, 5], dtx[:, 0]).then_inc(empty(("dt",)), 1)

            for b in range(HALVES):
                for t in range(TT):
                    wait_taken(dve, ("v", b, t))
                    last = nc.vector.bn_stats(vstat[:, t, b, :], v[:, t, b * W:(b + 1) * W])
            link(last)
            for t in range(TT):
                last = nc.vector.bn_aggr(vmean[:, t, :], vstat[:, t].rearrange("p a b -> p (a b)"))
            link(last)
            link(ts(ssq[:], vmean[:, :, 1], LN_EPS, None, ALU.add))
            nc.vector.reciprocal(ssq[:], ssq[:]).then_inc(v_var, 1)
            link(nc.vector.memset(sgu_wT[CHUNK:P, :, 0:CHUNK], 0.0))
            for h in range(2):
                name = ("sguw", h)
                wait_filled(dve, name)
                cp(sgu_wT[0:CHUNK, 4 * h:4 * h + 4, :], seg4(bank_of(name)[0:CHUNK, :]))
                cp(sgu_wT[CHUNK:P, 4 * h:4 * h + 4, CHUNK:P], seg4(bank_of(name)[CHUNK:P, :])[:, :, CHUNK:P]).then_inc(empty(name), 1)
            name = ("acs",)
            wait_filled(dve, name)
            both = bank_of(name)[:, 0:TT * 2 * HEADS].rearrange("p (c a h) -> p c a h", c=TT, a=2)
            link(cp(acs[:, :, 0, :], both[:, :, 0, :]))
            tt(acs[:, :, 1, :], both[:, :, 1, :], acs[:, :, 0, :], ALU.subtract).then_inc(acs_done, 1)
            dve.wait_ge(acs_done, 1)
            cp(dtx[:, 5], dtx[:, 0]).then_inc(empty(name), 1)

            def heads(ap):
                return ap.rearrange("p (h n) -> p h n", n=HEAD_DIM)

            def per_head(ap):
                return ap.unsqueeze(2).to_broadcast([P, ap.shape[1], HEAD_DIM])

            for c in range(TT):
                wait_taken(dve, ("xs", c, 0), ("xs", c, 1))
                tt(heads(xdt[:, c, :]), heads(xs[:, c, :]), per_head(dt[:, c, :]), ALU.mult).then_inc(xdt_done, 1)
            dve.wait_ge(edec_done, 1)
            dve.wait_ge(xdt_done, TT)
            tt(heads(xdte), heads(xdt[:, 0, :]), per_head(edec[:, 0, 1, :]), ALU.mult).then_inc(xdt_done, 1)
            for c in range(TT):
                tt(heads(xs[:, c, :]), heads(xs[:, c, :]), per_head(dskip[:]), ALU.mult)
            dve.wait_ge(v_rstd, 1)
            dve.wait_ge(ln_loaded, 32)
            for t in range(TT):
                last = ts(v[:, t, :], v[:, t, :], vmean[:, t, 0:1], rstd[:, t:t + 1], ALU.subtract, ALU.mult)
            link(last)
            for t in range(TT):
                last = tt(v[:, t, :], v[:, t, :], ln_g, ALU.mult)
            link(last)
            for t in range(TT):
                tt(v[:, t, :], v[:, t, :], ln_b, ALU.add).then_inc(v_done, 1)
            for c in range(TT):
                name = ("cb", c)
                wait_filled(dve, name)
                tt(cbm[:, c], seg4(bank_of(name)[:, :]), upper[:].unsqueeze(1).to_broadcast([P, GROUPS, P]),
                   ALU.mult).then_inc(empty(name), 1)
            wait_taken(dve, *all_of("u"))
            for c in range(TT):
                for h in range(2):
                    name = ("mix", c, h)
                    wait_filled(dve, name)
                    for i in range(4):
                        g = 4 * h + i
                        r = ROWS["sgu_b"] + g
                        cols = u[:, c, g * P:(g + 1) * P]
                        last = stt(cols, bank_of(name)[:, i * P:(i + 1) * P], paramT[:, r:r + 1], cols, ALU.add, ALU.mult)
                    last.then_inc(empty(name), 1)

            def segments(c, g):
                name = ("seg", c, g)
                wait_filled(dve, name)
                for r in range(HPG):
                    h = g * HPG + r
                    last = ts(decay[c][:, h, :], bank_of(name)[:, r * P:(r + 1) * P], acs[:, c, 0, h:h + 1], 0.0,
                              ALU.subtract, ALU.min)
                last.then_inc(empty(name), 1)

            def decays(c, g, n):
                dve.wait_ge(dexp_done, n + 1)
                d = decay[c][:, g * HPG:(g + 1) * HPG, :]
                tt(d, d, cbm[:, c, g, :].unsqueeze(1).to_broadcast([P, HPG, P]), ALU.mult).then_inc(decay_done, 1)

            wait_taken(dve, ("cb", 0), ("cb", 1))
            order = [(c, g) for c in range(TT) for g in range(GROUPS)]
            for i, cg in enumerate(order):
                segments(*cg)
                if i >= 2:
                    decays(*order[i - 2], i - 2)
            for i in (-2, -1):
                decays(*order[i], len(order) + i)
            for i, name in enumerate(all_of("z")):
                _, b, t = name
                dve.wait_ge(zsig_done, i + 1)
                cols = z[:, t, b * W:(b + 1) * W]
                tt(cols, cols, bank_of(name)[:, :], ALU.mult).then_inc(empty(name), 1)
            wait_taken(dve, *all_of("z"))

            def y_take(c, hf):
                name = ("yd", c, hf)
                cols = xs[:, c, hf * W:(hf + 1) * W]
                wait_filled(dve, name)
                tt(cols, cols, bank_of(name)[:, :], ALU.add).then_inc(empty(name), 1)
                wait_taken(dve, name)
                if c:
                    off = ("yo", hf)
                    tmp = xdte[:, hf * W:(hf + 1) * W]
                    wait_filled(dve, off)
                    tt(heads(tmp), heads(bank_of(off)[:, :]), per_head(edec[:, 1, 0, 8 * hf:8 * hf + 8]), ALU.mult).then_inc(empty(off), 1)
                    wait_taken(dve, off)
                    link(tt(cols, cols, tmp, ALU.add))

            for c in range(TT):
                for hf in range(2):
                    y_take(c, hf)
                tt(z[:, c, :], z[:, c, :], xs[:, c, :], ALU.mult).then_inc(y_done, 1)
            dve.wait_ge(yssq_done, TT)
            link(ts(yssq[:], yssq[:], 1.0 / GDIM, RMS_EPS, ALU.mult, ALU.add))
            nc.vector.reciprocal(yssq[:], yssq[:]).then_inc(yms_done, 1)
            dve.wait_ge(yrstd_done, 1)
            for t in range(TT):
                zg = z[:, t, :].rearrange("p (g n) -> p g n", g=GROUPS)
                tt(zg, zg, yssq[:, t, :].unsqueeze(2).to_broadcast([P, GROUPS, GDIM]), ALU.mult).then_inc(yb_done, 1)

            wait_taken(dve, *all_of("ga"), *all_of("gb"))
            for name in all_of("wa"):
                _, b, t = name
                cols = ga[:, t, b * W:(b + 1) * W]
                wait_filled(dve, name)
                tt(cols, cols, bank_of(name)[:, :], ALU.mult).then_inc(empty(name), 1)
            wait_taken(dve, *all_of("wa"))
            for t in range(TT):
                for h in range(2):
                    scaled(("ybT", t, h), ybT, ROWS["ssm"], t, h)
            for name in all_of("wb"):
                _, b, t = name
                cols = slice(b * W, (b + 1) * W)
                wait_filled(dve, name)
                tt(gb[:, t, cols], gb[:, t, cols], bank_of(name)[:, :], ALU.mult).then_inc(empty(name), 1)
                wait_taken(dve, name)
                tt(ga[:, t, cols], ga[:, t, cols], gb[:, t, cols], ALU.add).then_inc(merged, 1)
            for name in all_of("wo"):
                _, b, t = name
                cols = x[:, t, b * W:(b + 1) * W]
                wait_filled(dve, name)
                tt(cols, cols, bank_of(name)[:, :], ALU.add).then_inc(empty(name), 1)

            norm(1, xn)
            for t in range(TT):
                for h in range(2):
                    scaled(("fT", t, h), hT, ROWS["ffn"], t, h)

            name = ("logit",)
            wait_filled(dve, name)
            nc.vector.memset(lg[:, :, E:E + 4], BIG)
            nc.vector.memset(rep[:, :, TOPK:8], BIG)
            tt(lg[:, :, 0:E], bank_of(name)[:, 0:TT * E].rearrange("p (t e) -> p t e", t=TT),
               br[:].unsqueeze(1).to_broadcast([P, TT, E]), ALU.add).then_inc(empty(name), 1)
            wait_taken(dve, name)
            for t in range(TT):
                last = nc.vector.max(top[:, t, :], lg[:, t, 0:E])
            link(last)
            ts(ngm, top[:, :, 0], -1.0, None, ALU.mult).then_inc(neg_max, 1)
            link(cp(rep[:, :, 0:TOPK], top[:, :, 0:TOPK]))
            for t in range(TT):
                last = nc.vector.match_replace(lg2[:, t, :], rep[:, t, :], lg[:, t, :], -BIG)
            link(last)
            tt(mask, lg2[:, :, 0:E], lg[:, :, 0:E], ALU.not_equal).then_inc(mask_done, 1)
            nc.vector.memset(rj[:, :, E:NJ], -1.0)
            cp(onehot[:, 0:E], ident[0:E, 0:E])
            dve.wait_ge(mask_done, 1)
            dve.wait_ge(lexp_done, 1)
            link(tt(ex, ex, mask, ALU.mult))
            link(nc.vector.reduce_sum(gsum, ex, AX.X))
            link(nc.vector.reciprocal(gsum, gsum))
            tt(gj[:, :, 0:E], ex, gsum.unsqueeze(2).to_broadcast([P, TT, E]), ALU.mult).then_inc(gate_done, 1)
            name = ("rank",)
            wait_filled(dve, name)
            rank = bank_of(name)
            link(stt(rj[:, :, 0:E], rank[:, 0:TT * E].rearrange("p (t e) -> p t e", t=TT), 1.0, mask, ALU.add, ALU.mult))
            link(ts(rj[:, :, 0:E], rj[:, :, 0:E], -1.0, None, ALU.add))

            def select(j):
                for t in range(TT):
                    last = ts(sel[:, t, :], slot_id[:, 0:SLOTS], rj[:, t, bass.ds(j, 1)], None, ALU.is_equal)
                last.then_inc(sel_done, 1)

            def take_gathered():
                tt(xgT, YB[:, :].rearrange("p (k s) -> p k s", k=KT),
                   paramT[:, ROWS["ffn"]:ROWS["ffn"] + KT].unsqueeze(2).to_broadcast([P, KT, SLOTS]), ALU.mult).then_inc(xg_done, 1)

            select(0)
            link(cp(cnt, rank[0:1, 2 * E:3 * E]))
            link(ts(cov, cnt, float(SLOTS), None, ALU.is_gt))
            for m in (2, 3):
                link(stt(cov, cnt, float(m * SLOTS), cov, ALU.is_gt, ALU.add))
            link(nc.vector.reduce_sum(cnt[:, 0:1], cov, AX.X))
            cp(n_extra[:], cnt[:, 0:1]).then_inc(extra_done, 1)
            nc.vector.memset(selgT, 0.0).then_inc(selT_done, 1)
            wait_taken(dve, ("pT",))
            nc.vector.memset(y_sb, 0.0).then_inc(y_copied, 1)
            cp(dtx[:, 5], dtx[:, 0]).then_inc(empty(("rank",)), 1)
            dve.wait_ge(gateT_filled, 1)
            cp(gateT, TB[0:E, 0:TOKENS]).then_inc(gateT_done, 1)
            dve.wait_ge(gathered, 1)
            take_gathered()

            def expert(j, more):
                select(j + 1)
                ts(esel, ones[0:E, 0:SLOTS], onehot[:, bass.ds(j, 1)], None, ALU.mult)
                for t in range(TT):
                    last = ts(selg[:, t, :], slot_id[:], rj[:, t, bass.ds(j, 1)], gj[:, t, bass.ds(j, 1)],
                              ALU.is_equal, ALU.mult)
                last.then_inc(aux_done, 1)
                dve.wait_ge(hid_filled, j + 1)
                ts(g_sb, GLU[:, :], LIMIT, None, ALU.min).then_inc(g_done, 1)
                ts(lin_sb, LIN[:, :], LIMIT, -LIMIT, ALU.min, ALU.max).then_inc(loop_step, 1)
                dve.wait_ge(loop_step, 2 * j + 1)
                stt(act_sb, lin_sb, 1.0, g_sb, ALU.add, ALU.mult).then_inc(loop_step, 1)
                dve.wait_ge(loop_step, 2 * j + 2)
                dve.wait_ge(msig_done, j + 1)
                tt(act_sb, act_sb, sig_sb, ALU.mult).then_inc(actv_done, 1)
                dve.wait_ge(gathered, j + (2 + more))
                take_gathered()
                dve.wait_ge(actT_filled, j + 1)
                cp(actT, TB[:, :]).then_inc(actT_done, 1)
                dve.wait_ge(selT_filled, j + 1)
                cp(selgT.rearrange("p t s -> p (t s)"), TB[:, 0:TT * P]).then_inc(selT_done, 1)

            with dve.Fori(0, E) as j:
                expert(j, 0)
            n = dve.value_load(n_extra[0:1, 0:1], min_val=0, max_val=OVF - 1)
            with dve.If(n > 0):
                dve.wait_ge(ovf_mm, 1)
                olink(cp(ecnt[:, 0:1], TB[0:E, 0:1]))
                olink(ts(ecnt[:, 1:2], ecnt[:, 0:1], float(SLOTS), None, ALU.is_gt))
                olink(stt(ecnt[:, 1:2], ecnt[:, 0:1], 2.0 * SLOTS, ecnt[:, 1:2], ALU.is_gt, ALU.add))
                stt(ecnt[:, 1:2], ecnt[:, 0:1], 3.0 * SLOTS, ecnt[:, 1:2], ALU.is_gt, ALU.add).then_inc(ovf_dve, 1)
                dve.wait_ge(ovf_mm, 3)
                dve.wait_ge(ovf_dve, 1)
                olink(cp(ecnt[:, 2:3], TB[0:E, 1:2]))
                olink(tt(estart, ecnt[:, 2:3], ecnt[:, 1:2], ALU.subtract))
                olink(ts(ecnt[:, 3:4], estart, float(SLOTS), None, ALU.mult))
                olink(ts(ohtmp, slot_id[0:E, 0:OVF], estart, None, ALU.is_ge))
                stt(onehot[:, E:E + OVF], slot_id[0:E, 0:OVF], ecnt[:, 2:3], ohtmp, ALU.is_lt, ALU.mult).then_inc(ovf_dve, 1)
                ts(rankT, TB[0:E, P:P + TOKENS], ecnt[:, 3:4], None, ALU.add).then_inc(ovf_dve, 1)
                olink(ts(ofs, slot_id[:, 0:OVF], -float(SLOTS), -float(SLOTS), ALU.mult, ALU.add))
                dve.wait_ge(ovf_mm, 4)
                for t in range(TT):
                    tt(rj[:, t, E:E + OVF], TB[:, 384 + t * OVF:384 + (t + 1) * OVF], ofs, ALU.add)
                    last = cp(gj[:, t, E:E + OVF], TB[:, 416 + t * OVF:416 + (t + 1) * OVF])
                last.then_inc(ovf_dve, 1)
                cp(ids[:], TB[0:1, 448:448 + OVF]).then_inc(ovf_dve, 1)
                dve.wait_ge(ovf_dve, 5)
                select(E)
                dve.wait_ge(gathered, E + 2)
                take_gathered()
                with dve.Fori(0, n) as q:
                    expert(q + E, 1)

            dve.wait_ge(acc_done, 1)
            for t in range(TT):
                for dh in range(2):
                    cols = x[:, t, dh * W:(dh + 1) * W]
                    last = tt(cols, cols, ACC[t][dh][:, :], ALU.add)
                last.then_inc(x2_done, 1)
            norm(2, xn)
            for t in range(TT):
                for h in range(2):
                    gain = paramT[:, ROWS["ple"] + 4 * h:ROWS["ple"] + 4 * h + 4].unsqueeze(2).to_broadcast([P, 4, P])
                    dve.wait_ge(tail_filled, 2 * t + h + 1)
                    tt(hT[:, 4 * h:4 * h + 4, t * P:(t + 1) * P], seg4(banks[4 + 2 * t + h][:, :]), gain, ALU.mult).then_inc(tail_hT, 1)
            for b in range(HALVES):
                for t in range(TT):
                    cols = slice(b * W, (b + 1) * W)
                    dve.wait_ge(tail_sig, 2 * b + t + 1)
                    link(tt(v[:, t, cols], v[:, t, cols], yproj[:, t, cols], ALU.mult))
                    last = tt(x[:, t, cols], x[:, t, cols], v[:, t, cols], ALU.add)
                    if b == HALVES - 1:
                        last.then_inc(x3_done, 1)
            norm(3, None)
            for t in range(TT):
                stt(xn[:, t, :], x[:, t, :], rstd[:, t:t + 1], fnorm, ALU.mult, ALU.mult).then_inc(out_ready, 1)


_INS = ["x", "p", "mix_norm", "w_in", "sgu_ln_g", "sgu_ln_b", "sgu_w", "sgu_b", "conv_w", "conv_b", "dt_bias", "a_log",
        "d_skip", "ssm_norm", "w_branch_a", "w_branch_b", "w_out", "ffn_norm", "w_router", "b_router", "w1", "b1", "w2",
        "b2", "ple_norm", "w_ple_gate", "w_ple_proj", "final_norm"]
_OUTS = [((1, TOKENS, D), "float32")]


def kernel(**inputs):
    import numpy as _np
    import concourse.bacc as _bacc
    from concourse import mybir as _mybir
    from concourse.bass_utils import run_bass_kernel_spmd as _run

    nc = _bacc.Bacc("TRN2", target_bir_lowering=False, num_devices=1)
    arrays, args = {}, []
    for name in _INS:
        a = _np.ascontiguousarray(inputs[name])
        arrays[f"in_{name}_dram"] = a
        args.append(nc.dram_tensor(f"in_{name}_dram", a.shape, _mybir.dt.from_np(a.dtype), kind="ExternalInput").ap())
    for i, (shape, dtype) in enumerate(_OUTS):
        dt = _mybir.dt.from_np(_np.dtype(dtype))
        args.append(nc.dram_tensor(f"out_{i}_dram", shape, dt, kind="ExternalOutput").ap())
    build(nc, *args)
    r = _run(nc, [arrays], core_ids=[0])
    return r.results[0]["out_0_dram"]
```

```python
from contextlib import ExitStack

import concourse.bass as bass
from concourse import mybir

FP32 = mybir.dt.float32
FP32R = mybir.dt.float32r
I32 = mybir.dt.int32
ALU = mybir.AluOpType
ACT = mybir.ActivationFunctionType
AX = mybir.AxisListType

P = 128
D = 1024
TOKENS = 256
TT = TOKENS // P
KT = D // P
W = 512
HALVES = D // W
CHUNK = 64
SGU_HEADS = 8
HEADS = 16
HEAD_DIM = 64
GROUPS = 4
HPG = HEADS // GROUPS
GDIM = D // GROUPS
CONV_TILES = 16
TAPS = 4
B0, C0 = 8, 12
PLE = 256
E = 32
TOPK = 4
F = 1024
LIMIT = 7.0
ALPHA = 1.702
RMS_EPS = 1e-6
LN_EPS = 1e-5
BIG = 3.0e38

OFF_U, OFF_V, OFF_Z, OFF_XBC = 0, D, 2 * D, 3 * D
OFF_DT = OFF_XBC + CONV_TILES * P
OFF_GA = OFF_DT + HEADS
OFF_GB = OFF_GA + D

SLOTS = 64
OVF = TOKENS * TOPK // SLOTS
W1C, W2C = KT, KT // 2
NCH = W1C + W2C

HALF = KT * TOKENS
NATURAL = ("v", "u", "z", "ga", "gb", "wa", "wb", "wo", "pg")
WEIGHTS = [("xbc", b, j) for b in range(4) for j in range(2)]
WEIGHTS += [(n, b, kh) for n in NATURAL for b in range(2) for kh in range(2)]
HALF_OF = {name: i for i, name in enumerate(WEIGHTS)}
NB = 4
FIRST_WA = HALF_OF["wa", 0, 0]
SPLIT = HALF_OF["pg", 0, 0]


def unit_order():
    two = [(a, b) for a in range(TT) for b in range(2)]
    nat = lambda n: [(n, b, t) for b in range(HALVES) for t in range(TT)]
    u = [("param",)]
    u += [("xT", t, h) for t, h in two]
    u += [("xbc", b, j) for b in range(4) for j in range(2)]
    u += [("dt",)]
    u += nat("v")
    u += [("sguw", h) for h in range(2)]
    u += [("acs",)] + [("xs", c, h) for c, h in two] + [("bn",)]
    u += nat("u")
    u += [("cb", c) for c in range(TT)]
    u += [("mix", c, h) for c, h in two]
    u += [("seg", c, g) for c in range(TT) for g in range(GROUPS)]
    u += nat("z")
    u += [("state", h) for h in range(2)]
    u += [("yd", 0, 0), ("yd", 0, 1), ("yd", 1, 0), ("yo", 0), ("yd", 1, 1), ("yo", 1)]
    u += nat("ga") + [("yaT", t, h) for t, h in two] + nat("gb")
    u += [("wa", 0, t) for t in range(TT)] + [("ybT", t, h) for t, h in two] + [("wa", 1, t) for t in range(TT)]
    u += nat("wb")
    u += [("pT",)] + [("pp", 0, t) for t in range(TT)]
    u += [("mT", t, h) for t, h in two] + nat("wo")
    u += [("pp", 1, t) for t in range(TT)]
    u += [("fT", t, h) for t, h in two]
    u += [("logit",), ("rank",)]
    return u


UNITS = unit_order()
UNIT = {name: i for i, name in enumerate(UNITS)}
BANKS = 8
ROWS = {"mix": 0, "ffn": 8, "ple": 16, "ssm": 24, "sgu_b": 32, "conv_b": 40, "conv_w": 56}
NROWS = 56 + TAPS * CONV_TILES


def build(nc, x_in, p_in, mix_norm, w_in, sgu_ln_g, sgu_ln_b, sgu_w, sgu_b, conv_w, conv_b, dt_bias,
          a_log, d_skip, ssm_norm, w_branch_a, w_branch_b, w_out, ffn_norm, w_router, b_router,
          w1, b1, w2, b2, ple_norm, w_ple_gate, w_ple_proj, final_norm, out):
    ctx = ExitStack()
    with ctx:
        def sb(name, shape, dt=FP32):
            return ctx.enter_context(nc.sbuf_tensor(name, shape, dt))

        def sem(name):
            return ctx.enter_context(nc.semaphore(name))

        def alias(name, at, shape, dt=FP32R):
            with ExitStack() as inner:
                if at:
                    inner.enter_context(nc.sbuf_tensor(f"below_{name}", [P, at // 4], FP32))
                return inner.enter_context(nc.sbuf_tensor(name, shape, dt))

        X_AT, HT_AT = 0, TT * D * 4
        BLK_AT = HT_AT + KT * TOKENS * 4
        RING_AT = BLK_AT + NB * HALF * 4
        CHUNK_BYTES = 2 * F * 4
        a_hi = alias("a_hi", X_AT, [P, KT, TOKENS])
        a_lo = alias("a_lo", HT_AT, [P, KT, TOKENS])
        b_hi = alias("b_hi", RING_AT + 6 * CHUNK_BYTES, [P, KT, TOKENS])
        b_lo = alias("b_lo", RING_AT + 7 * CHUNK_BYTES, [P, KT, TOKENS])
        blk_hi1 = alias("blk_hi1", RING_AT, [P, NB, HALF])
        blk_hi2 = alias("blk_hi2", RING_AT + 8 * CHUNK_BYTES, [P, NB, HALF])
        blk_lo = alias("blk_lo", BLK_AT, [P, NB, HALF])
        wdt_hi = alias("wdt_hi", RING_AT + 4 * CHUNK_BYTES + 1792 * 4, [P, KT * HEADS])
        wdt_lo = alias("wdt_lo", RING_AT + 4 * CHUNK_BYTES + 1920 * 4, [P, KT * HEADS])

        x = sb("x", [P, TT, D])
        hT = sb("hT", [P, KT, TOKENS])
        blk = sb("blk", [P, NB, HALF])
        wring = sb("wring", [P, NCH, 2 * F])
        xbcT = sb("xbcT", [P, CONV_TILES, TOKENS])
        v = sb("v", [P, TT, D])
        u = sb("u", [P, TT, D])
        z = sb("z", [P, TT, D])
        ga = sb("ga", [P, TT, D])
        gb = sb("gb", [P, TT, D])
        ident = sb("ident", [P, P])
        upper = sb("upper", [P, P])
        strict = sb("strict", [P, P])
        ones = sb("ones", [P, P])
        slot_id = sb("slot_id", [P, 2 * SLOTS])
        row_id = sb("row_id", [E, 1])
        paramT = sb("paramT", [P, NROWS])
        wr = sb("wr", [P, KT, E])
        br = sb("br", [P, E])
        dtb = sb("dtb", [P, HEADS])
        alog = sb("alog", [P, HEADS])
        dskip = sb("dskip", [P, HEADS])
        ssq = sb("ssq", [P, TT])
        rstd = sb("rstd", [P, TT])
        vstat = sb("vstat", [P, TT, 2, 6])
        vmean = sb("vmean", [P, TT, 2])
        yssq = sb("yssq", [P, TT, GROUPS])
        dtx = sb("dtx", [P, 6, TT, HEADS])
        dt = sb("dt", [P, TT, HEADS])
        adt = sb("adt", [P, TT, HEADS])
        acs = sb("acs", [P, TT, 2, HEADS])
        edec = sb("edec", [P, TT, 2, HEADS])
        n_extra = sb("n_extra", [1, 1], I32)
        ids = sb("ids", [1, OVF], I32)

        def chunk(i, a=0, n=2 * F):
            return wring[:, i, a:a + n]

        bnat = chunk(4, 0, 512).rearrange("p (g n) -> p g n", g=GROUPS)
        cbm = chunk(4, 512, 1024).rearrange("p (c g q) -> p c g q", c=TT, g=GROUPS)
        prow = chunk(4, 1536, P)
        wdt = chunk(4, 1664, KT * HEADS).rearrange("p (k h) -> p k h", k=KT)
        state = chunk(5, 0, D)
        xdte = chunk(5, D, D)
        decay = [chunk(6 + c).rearrange("p (h q) -> p h q", h=HEADS) for c in range(TT)]
        xdt = chunk(8).rearrange("p (c n) -> p c n", c=TT)
        xs = chunk(9).rearrange("p (c n) -> p c n", c=TT)
        ln_g, ln_b = chunk(10, 0, D), chunk(10, D, D)
        sgu_nat = chunk(11, 0, D).rearrange("p (g s) -> p g s", g=SGU_HEADS)
        sgu_wT = chunk(11, D, D).rearrange("p (g s) -> p g s", g=SGU_HEADS)

        def flat(t):
            return t[:, :, :].rearrange("p a b -> p (a b)")

        ybT = xbcT[:, 0:KT, :]
        wpp = flat(v).rearrange("p (k n) -> p k n", k=PLE // P)
        yproj = u
        xc = flat(xbcT)
        junk = xc[:, 0:TT * D].rearrange("p (t n) -> p t n", t=TT)
        pT = xc[:, 2048:2560].rearrange("p (k t) -> p k t", k=PLE // P)
        p_nat = xc[:, 2560:3072].rearrange("p (t n) -> p t n", t=TT)
        fnorm = z[:, 0, :]
        b2_all = z[0:E, 1, :]
        b1_all = flat(gb)[0:E, :]
        xn = ga
        g_sb, sig_sb, lin_sb, act_sb = (xc[:, i * W:(i + 1) * W] for i in range(4))
        actT = xc[:, 2048:2560]
        y_sb = xc[:, 2560:3072]
        sel = xc[:, 3072:3200].rearrange("p (t s) -> p t s", t=TT)
        selg = xc[:, 3200:3456].rearrange("p (t s) -> p t s", t=TT)
        selgT = xc[:, 3456:3712].rearrange("p (t s) -> p t s", t=TT)
        esel = xc[0:E, 3712:3776]
        hc = flat(hT)
        xgT = hc[:, 0:512].rearrange("p (k s) -> p k s", k=KT)
        NJ = E + OVF + 1

        def table(at, n, rows=P):
            return hc[0:rows, at:at + n]

        rj = table(512, TT * NJ).rearrange("p (t j) -> p t j", t=TT)
        gj = table(640, TT * NJ).rearrange("p (t j) -> p t j", t=TT)
        onehot = table(768, E + OVF, E)
        gateT = table(832, TOKENS, E)
        rankT = table(1088, TOKENS, E)
        lg = table(1344, TT * (E + 4)).rearrange("p (t j) -> p t j", t=TT)
        lg2 = table(1424, TT * (E + 4)).rearrange("p (t j) -> p t j", t=TT)
        mask = table(1504, TT * E).rearrange("p (t j) -> p t j", t=TT)
        ex = table(1568, TT * E).rearrange("p (t j) -> p t j", t=TT)
        top = table(1632, TT * 8).rearrange("p (t j) -> p t j", t=TT)
        rep = table(1648, TT * 8).rearrange("p (t j) -> p t j", t=TT)
        ngm = table(1664, TT)
        gsum = table(1668, TT)
        cnt = table(1672, E, 1)
        cov = table(1704, E, 1)
        ecnt = table(1736, 4, E)
        estart = table(1744, 1, E)
        ohtmp = table(1748, OVF, E)
        ofs = table(1764, OVF)

        banks = [ctx.enter_context(nc.psum_tensor(f"bank{i}", [P, W], FP32)) for i in range(BANKS)]
        ACC = [[banks[t * 2 + dh] for dh in range(2)] for t in range(TT)]
        GLU, LIN, YB, TB = banks[4:8]

        filled = [sem(f"filled{i}") for i in range(BANKS)]
        drained = [sem(f"drained{i}") for i in range(BANKS)]
        blk_loaded = [sem(f"blk_loaded{i}") for i in range(NB)]
        blk_high = sem("blk_high")
        blk_low = sem("blk_low")
        row_half_used = sem("row_half_used")
        wdt_high = sem("wdt_high")
        wdt_low = sem("wdt_low")
        act_high = sem("act_high")
        act_low = sem("act_low")
        x_reloaded = sem("x_reloaded")
        x_loaded = [sem(f"x_loaded{i}") for i in range(TT)]
        rows_loaded = sem("rows_loaded")
        small_loaded = sem("small_loaded")
        sguw_loaded = sem("sguw_loaded")
        ln_loaded = sem("ln_loaded")
        late_loaded = sem("late_loaded")
        wpp_loaded = sem("wpp_loaded")
        p_loaded = sem("p_loaded")
        consts = sem("consts")
        ssq_done = sem("ssq_done")
        ms_done = sem("ms_done")
        rstd_done = sem("rstd_done")
        xn_done = sem("xn_done")
        tap_done = sem("tap_done")
        conv_done = sem("conv_done")
        sig_done = sem("sig_done")
        dt_neg = sem("dt_neg")
        dt_exp = sem("dt_exp")
        dt_one = sem("dt_one")
        dt_ln = sem("dt_ln")
        adt_done = sem("adt_done")
        acs_done = sem("acs_done")
        edec_done = sem("edec_done")
        xdt_done = sem("xdt_done")
        dexp_done = sem("dexp_done")
        decay_done = sem("decay_done")
        v_var = sem("v_var")
        v_rstd = sem("v_rstd")
        v_done = sem("v_done")
        zsig_done = sem("zsig_done")
        y_done = sem("y_done")
        yssq_done = sem("yssq_done")
        yms_done = sem("yms_done")
        yrstd_done = sem("yrstd_done")
        yb_done = sem("yb_done")
        merged = sem("merged")
        dve_step = sem("dve_step")
        pool_step = sem("pool_step")
        neg_max = sem("neg_max")
        lexp_done = sem("lexp_done")
        mask_done = sem("mask_done")
        gate_done = sem("gate_done")
        gateT_filled = sem("gateT_filled")
        gateT_done = sem("gateT_done")
        extra_done = sem("extra_done")
        loaded = [sem(f"loaded{i}") for i in range(NCH)]
        chunk_used = sem("chunk_used")
        sel_done = sem("sel_done")
        aux_done = sem("aux_done")
        gathered = sem("gathered")
        xg_done = sem("xg_done")
        hid_filled = sem("hid_filled")
        g_done = sem("g_done")
        msig_done = sem("msig_done")
        actv_done = sem("actv_done")
        actT_filled = sem("actT_filled")
        actT_done = sem("actT_done")
        y_copied = sem("y_copied")
        selT_filled = sem("selT_filled")
        selT_done = sem("selT_done")
        loop_step = sem("loop_step")
        ovf_mm = sem("ovf_mm")
        ovf_step = sem("ovf_step")
        ovf_dve = sem("ovf_dve")
        acc_done = sem("acc_done")
        x2_done = sem("x2_done")
        x3_done = sem("x3_done")
        tail_filled = sem("tail_filled")
        tail_hT = sem("tail_hT")
        tail_gate = sem("tail_gate")
        tail_sig = sem("tail_sig")
        out_ready = sem("out_ready")
        stored = sem("stored")

        def bank_of(name):
            return banks[UNIT[name] % BANKS]

        def wait_filled(eng, name):
            i = UNIT[name]
            eng.wait_ge(filled[i % BANKS], i // BANKS + 1)

        def wait_empty(eng, name):
            i = UNIT[name]
            if i >= BANKS:
                eng.wait_ge(drained[i % BANKS], i // BANKS)

        def wait_taken(eng, *names):
            for name in names:
                i = UNIT[name]
                eng.wait_ge(drained[i % BANKS], i // BANKS + 1)

        def all_of(kind):
            return [n for n in UNITS if n[0] == kind]

        def full(name):
            return filled[UNIT[name] % BANKS]

        def empty(name):
            return drained[UNIT[name] % BANKS]

        def weights_used(eng, i):
            kind, b, part = WEIGHTS[i]
            if kind == "xbc":
                wait_filled(eng, (kind, b, part))
            elif part == 0:
                eng.wait_ge(row_half_used, 2 * NATURAL.index(kind) + b + 1)
            else:
                wait_filled(eng, (kind, b, 1))

        def high(i):
            return (blk_hi1 if i < FIRST_WA else blk_hi2)[:, i % NB, :]

        def seg4(ap):
            return ap.rearrange("p (a b) -> p a b", b=P)

        def bcast(ap, shape):
            return ap.to_broadcast(shape)

        block = ctx.enter_context(nc.Block())

        @block.sync
        def _(sp):
            def load_half(i):
                kind, b, part = WEIGHTS[i]
                if kind == "xbc":
                    at = OFF_XBC + (2 * b + part) * TOKENS
                    src = w_in[0, :, at:at + TOKENS]
                else:
                    src, off = {"v": (w_in, OFF_V), "u": (w_in, OFF_U), "z": (w_in, OFF_Z), "ga": (w_in, OFF_GA),
                                "gb": (w_in, OFF_GB), "wa": (w_branch_a, 0), "wb": (w_branch_b, 0), "wo": (w_out, 0),
                                "pg": (w_ple_gate, 0)}[kind]
                    src = src[0, part * W:(part + 1) * W, off + b * W:off + (b + 1) * W]
                src = src.rearrange("(k p) n -> p k n", p=P)
                dst = blk[:, i % NB, :].rearrange("p (k n) -> p k n", k=src.shape[1])
                sp.dma_start(dst, src).then_inc(blk_loaded[i % NB], 16)

            def load(dst, src, done):
                sp.dma_start(dst, src).then_inc(done, 16)

            rows = lambda a: a.rearrange("a (k p) -> (a k) p", p=P)
            vec = lambda a: a.rearrange("a n -> (a n)").partition_broadcast(P)
            for t in range(TT):
                load(x[:, t, :], x_in[0, t * P:(t + 1) * P, :], x_loaded[t])
            load_half(0)
            for key, src in (("mix", rows(mix_norm)), ("ffn", rows(ffn_norm)), ("ple", rows(ple_norm)),
                             ("ssm", rows(ssm_norm)), ("sgu_b", sgu_b[0]), ("conv_b", rows(conv_b)),
                             ("conv_w", rows(conv_w[0]))):
                r = ROWS[key]
                load(prow[r:r + src.shape[0], :], src, rows_loaded)
            for i in range(1, NB):
                load_half(i)
            load(wdt, w_in[0, :, OFF_DT:OFF_DT + HEADS].rearrange("(k p) n -> p k n", p=P), small_loaded)
            load(dtb[:], vec(dt_bias), small_loaded)
            load(alog[:], vec(a_log), small_loaded)
            load(dskip[:], vec(d_skip), small_loaded)
            load(wr[:], w_router[0].rearrange("(k p) n -> p k n", p=P), small_loaded)
            load(br[:], vec(b_router), small_loaded)
            load(sgu_nat, sgu_w[0].rearrange("g t s -> t g s"), sguw_loaded)
            load(ln_g, vec(sgu_ln_g), ln_loaded)
            load(ln_b, vec(sgu_ln_b), ln_loaded)

            def chunk_src(e, c):
                if c < W1C:
                    return w1[0, e, c * P:(c + 1) * P, :]
                r = (c - W1C) * 2 * P
                return w2[0, e, r:r + 2 * P, :].rearrange("(k p) n -> p k n", p=P)

            def chunk_dst(c):
                if c < W1C:
                    return wring[:, c, :]
                return wring[:, c, :].rearrange("p (k n) -> p k n", k=2)

            def load_chunk(c):
                sp.dma_start(chunk_dst(c), chunk_src(0, c)).then_inc(loaded[c], 16)

            for i in range(NB, SPLIT):
                weights_used(sp, i - NB)
                load_half(i)
                if i == HALF_OF["gb", 0, 0]:
                    wait_filled(sp, ("yo", 1))
                    load(p_nat, p_in[0, 0].rearrange("(t p) n -> p t n", p=P), p_loaded)
                    wait_filled(sp, ("mix", 1, 1))
                    load(wpp, w_ple_proj[0].rearrange("(k p) n -> p k n", p=P), wpp_loaded)
                if FIRST_WA <= i < FIRST_WA + NB:
                    load_chunk(i - FIRST_WA)
                if FIRST_WA + NB <= i < FIRST_WA + NB + 2:
                    sp.wait_ge(y_done, TT)
                    load_chunk(i - FIRST_WA)
                if i == HALF_OF["wb", 1, 1]:
                    wait_filled(sp, ("ybT", 1, 1))
                    load(fnorm, final_norm.partition_broadcast(P), late_loaded)
                    load(b2_all, b2[0], late_loaded)
            for t in range(TT):
                load(x[:, t, :], x_in[0, t * P:(t + 1) * P, :], x_reloaded)
            sp.wait_ge(merged, 4)
            load(b1_all, b1[0], late_loaded)
            for i in range(SPLIT, len(WEIGHTS)):
                weights_used(sp, i - NB)
                if i == len(WEIGHTS) - 1:
                    load_chunk(6)
                    load_chunk(7)
                load_chunk(8 + i - SPLIT)
                load_half(i)

            with sp.Fori(1, E) as j:
                for c in range(NCH):
                    sp.wait_ge(chunk_used, NCH * j - NCH + (c + 1))
                    sp.dma_start(chunk_dst(c), chunk_src(j, c)).then_inc(loaded[c], 16)
            sp.wait_ge(extra_done, 1)
            n = sp.value_load(n_extra[0:1, 0:1], min_val=0, max_val=OVF - 1)
            with sp.If(n > 0):
                sp.wait_ge(ovf_dve, 5)
                with sp.Fori(0, n) as q:
                    e = sp.value_load(ids[0:1, bass.ds(q, 1)], min_val=0, max_val=E - 1)
                    for c in range(NCH):
                        sp.wait_ge(chunk_used, NCH * q + (NCH * (E - 1) + c + 1))
                        sp.dma_start(chunk_dst(c), chunk_src(e, c)).then_inc(loaded[c], 16)
            for t in range(TT):
                sp.wait_ge(out_ready, t + 1)
                sp.dma_start(out[0, t * P:(t + 1) * P, :], xn[:, t, :]).then_inc(stored, 16)
            sp.wait_ge(stored, 16 * TT)

        @block.gpsimd
        def _(pool):
            nc.gpsimd.memset(ident[:], 0.0)
            nc.gpsimd.memset(upper[:], 1.0)
            nc.gpsimd.memset(strict[:], 1.0)
            nc.gpsimd.memset(ones[:], 1.0)
            nc.gpsimd.iota(slot_id[:].rearrange("p (a s) -> p a s", a=2), pattern=[[0, 2], [1, SLOTS]], base=0,
                           channel_multiplier=0, allow_small_or_imprecise_dtypes=True)
            nc.gpsimd.iota(row_id[:], pattern=[[0, 1]], base=0, channel_multiplier=1,
                           allow_small_or_imprecise_dtypes=True).then_inc(pool_step, 1)
            pool.wait_ge(pool_step, 1)
            nc.gpsimd.affine_select(out=ident[:], in_=ident[:], compare_op=ALU.not_equal, fill=1.0, base=0,
                                    pattern=[[-1, P]], channel_multiplier=1)
            nc.gpsimd.affine_select(out=upper[:], in_=upper[:], compare_op=ALU.is_ge, fill=0.0, base=0,
                                    pattern=[[1, P]], channel_multiplier=-1)
            nc.gpsimd.affine_select(out=strict[:], in_=strict[:], compare_op=ALU.is_ge, fill=0.0, base=-1,
                                    pattern=[[1, P]], channel_multiplier=-1).then_inc(consts, 1)

            def subtract(dst, raw, hi, done):
                nc.gpsimd.tensor_tensor(dst, raw, hi.bitcast(FP32), ALU.subtract).then_inc(done, 1)

            for i in range(SPLIT):
                if i == HALF_OF["xbc", 3, 0]:
                    pool.wait_ge(wdt_high, 1)
                    subtract(wdt_lo[:], wdt.rearrange("p k h -> p (k h)"), wdt_hi[:], wdt_low)
                pool.wait_ge(blk_high, i + 1)
                subtract(blk_lo[:, i % NB, :], blk[:, i % NB, :], high(i), blk_low)

        @block.tensor
        def _(pe):
            mm = nc.tensor.matmul

            def transposes(name, parts):
                wait_empty(pe, name)
                bank = bank_of(name)
                for i, part in enumerate(parts):
                    k, m = part.shape
                    last = nc.tensor.transpose(bank[0:m, i * P:i * P + k], part, ident[0:k, 0:k])
                last.then_inc(full(name), 1)

            def dense(name, lhsT, rhs):
                wait_empty(pe, name)
                n = len(lhsT)
                for k in range(n):
                    last = mm(bank_of(name)[:, :], lhsT[k], rhs[k], start=(k == 0), stop=(k == n - 1))
                last.then_inc(full(name), 1)

            def three(out, lhs, rhs, start, stop):
                mm(out, lhs[1], rhs[0], start=start, stop=False)
                mm(out, lhs[0], rhs[0], start=False, stop=False)
                return mm(out, lhs[0], rhs[1], start=False, stop=stop)

            def natural(kind, hi, lo, blocks=range(HALVES)):
                for b in blocks:
                    for t in range(TT):
                        wait_empty(pe, (kind, b, t))
                    for kh in range(2):
                        i = HALF_OF[kind, b, kh]
                        pe.wait_ge(blk_low, i + 1)
                        for t in range(TT):
                            for kk in range(4):
                                k = 4 * kh + kk
                                cols = slice(t * P, (t + 1) * P)
                                last = three(bank_of((kind, b, t))[:, :], (hi[:, k, cols], lo[:, k, cols]),
                                             (high(i)[:, kk * W:(kk + 1) * W], blk_lo[:, i % NB, kk * W:(kk + 1) * W]),
                                             k == 0, k == KT - 1)
                            if kh == 1:
                                last.then_inc(full((kind, b, t)), 1)
                        if kh == 0:
                            last.then_inc(row_half_used, 1)

            pe.wait_ge(consts, 1)
            pe.wait_ge(rows_loaded, 16 * 7)
            transposes(("param",), [prow[0:NROWS, :]])
            for t in range(TT):
                pe.wait_ge(xn_done, t + 1)
                for h in range(2):
                    transposes(("xT", t, h), [v[:, t, (4 * h + i) * P:(4 * h + i + 1) * P] for i in range(4)])

            pe.wait_ge(act_low, 4)
            for b in range(4):
                for j in range(2):
                    i = HALF_OF["xbc", b, j]
                    name = ("xbc", b, j)
                    wait_empty(pe, name)
                    pe.wait_ge(blk_low, i + 1)
                    for c in range(2):
                        for k in range(KT):
                            cols = slice(k * TOKENS + c * P, k * TOKENS + (c + 1) * P)
                            last = three(bank_of(name)[:, c * TOKENS:(c + 1) * TOKENS],
                                         (high(i)[:, cols], blk_lo[:, i % NB, cols]), (a_hi[:, k, :], a_lo[:, k, :]),
                                         k == 0, k == KT - 1)
                    last.then_inc(full(name), 1)
            pe.wait_ge(wdt_low, 1)
            wait_empty(pe, ("dt",))
            for t in range(TT):
                for k in range(KT):
                    cols, heads = slice(t * P, (t + 1) * P), slice(k * HEADS, (k + 1) * HEADS)
                    last = three(bank_of(("dt",))[:, t * HEADS:(t + 1) * HEADS], (a_hi[:, k, cols], a_lo[:, k, cols]),
                                 (wdt_hi[:, heads], wdt_lo[:, heads]), k == 0, k == KT - 1)
            last.then_inc(full(("dt",)), 1)

            natural("v", a_hi, a_lo)
            pe.wait_ge(sguw_loaded, 16)
            for h in range(2):
                transposes(("sguw", h), [sgu_nat[:, 4 * h + i, :] for i in range(4)])

            pe.wait_ge(adt_done, 1)
            wait_empty(pe, ("acs",))
            for c in range(TT):
                mm(bank_of(("acs",))[:, c * 2 * HEADS:c * 2 * HEADS + HEADS], upper[:], adt[:, c, :], start=True, stop=True)
                last = mm(bank_of(("acs",))[:, c * 2 * HEADS + HEADS:(c + 1) * 2 * HEADS], ones[:], adt[:, c, :],
                          start=True, stop=True)
            last.then_inc(full(("acs",)), 1)
            wait_taken(pe, *all_of("xbc"))
            for c in range(TT):
                for h in range(2):
                    transposes(("xs", c, h), [xbcT[:, 4 * h + i, c * P:(c + 1) * P] for i in range(4)])
            transposes(("bn",), [xbcT[:, B0 + g, 0:P] for g in range(GROUPS)])
            natural("u", a_hi, a_lo)
            for c in range(TT):
                name = ("cb", c)
                wait_empty(pe, name)
                for g in range(GROUPS):
                    last = mm(bank_of(name)[:, g * P:(g + 1) * P], xbcT[:, B0 + g, c * P:(c + 1) * P],
                              xbcT[:, C0 + g, c * P:(c + 1) * P], start=True, stop=True)
                last.then_inc(full(name), 1)
            pe.wait_ge(v_done, TT)
            wait_taken(pe, *all_of("sguw"))
            for c in range(TT):
                for h in range(2):
                    name = ("mix", c, h)
                    wait_empty(pe, name)
                    for i in range(4):
                        g = 4 * h + i
                        last = mm(bank_of(name)[:, i * P:(i + 1) * P], sgu_wT[:, g, :], v[:, c, g * P:(g + 1) * P],
                                  start=True, stop=True)
                    last.then_inc(full(name), 1)
            for c in range(TT):
                for g in range(GROUPS):
                    name = ("seg", c, g)
                    wait_empty(pe, name)
                    for r in range(HPG):
                        h = g * HPG + r
                        last = mm(bank_of(name)[:, r * P:(r + 1) * P], bcast(adt[:, c, h:h + 1], [P, P]), upper[:],
                                  start=True, stop=True)
                    last.then_inc(full(name), 1)
            natural("z", a_hi, a_lo)
            pe.wait_ge(xdt_done, 3)
            wait_taken(pe, ("bn",))
            for hf in range(2):
                name = ("state", hf)
                wait_empty(pe, name)
                for i in range(2):
                    g = 2 * hf + i
                    last = mm(bank_of(name)[:, i * GDIM:(i + 1) * GDIM], bnat[:, g, :], xdte[:, g * GDIM:(g + 1) * GDIM],
                              start=True, stop=True)
                last.then_inc(full(name), 1)

            def y_diag(c, hf):
                name = ("yd", c, hf)
                pe.wait_ge(decay_done, c * GROUPS + 2 * hf + 2)
                wait_empty(pe, name)
                for i in range(8):
                    h = 8 * hf + i
                    last = mm(bank_of(name)[:, i * HEAD_DIM:(i + 1) * HEAD_DIM], decay[c][:, h, :],
                              xdt[:, c, h * HEAD_DIM:(h + 1) * HEAD_DIM], start=True, stop=True)
                last.then_inc(full(name), 1)

            def y_off(hf):
                name = ("yo", hf)
                wait_taken(pe, ("state", hf))
                wait_empty(pe, name)
                for i in range(2):
                    g = 2 * hf + i
                    last = mm(bank_of(name)[:, i * GDIM:(i + 1) * GDIM], xbcT[:, C0 + g, P:2 * P],
                              state[:, g * GDIM:(g + 1) * GDIM], start=True, stop=True)
                last.then_inc(full(name), 1)

            y_diag(0, 0)
            y_diag(0, 1)
            y_diag(1, 0)
            y_off(0)
            y_diag(1, 1)
            y_off(1)
            natural("ga", a_hi, a_lo)
            wait_taken(pe, *all_of("mix"))
            for t in range(TT):
                for h in range(2):
                    transposes(("yaT", t, h), [u[:, t, (4 * h + i) * P:(4 * h + i + 1) * P] for i in range(4)])
            natural("gb", a_hi, a_lo)
            wait_taken(pe, *all_of("yaT"))
            natural("wa", b_hi, b_lo, [0])
            pe.wait_ge(yb_done, 2)
            for t in range(TT):
                for h in range(2):
                    transposes(("ybT", t, h), [z[:, t, (4 * h + i) * P:(4 * h + i + 1) * P] for i in range(4)])
            natural("wa", b_hi, b_lo, [1])
            pe.wait_ge(act_low, 8)
            natural("wb", a_hi, a_lo)
            pe.wait_ge(p_loaded, 16)
            transposes(("pT",), [p_nat[:, t, k * P:(k + 1) * P] for k in range(2) for t in range(TT)])
            pe.wait_ge(wpp_loaded, 16)
            wait_taken(pe, ("pT",))

            def embed(b):
                for t in range(TT):
                    dense(("pp", b, t), [pT[:, k, t * P:(t + 1) * P] for k in range(2)],
                          [wpp[:, k, b * W:(b + 1) * W] for k in range(2)])

            embed(0)
            for t in range(TT):
                pe.wait_ge(merged, TT + t + 1)
                for h in range(2):
                    transposes(("mT", t, h), [ga[:, t, (4 * h + i) * P:(4 * h + i + 1) * P] for i in range(4)])
            wait_taken(pe, *all_of("mT"))
            natural("wo", b_hi, b_lo)
            embed(1)
            for t in range(TT):
                pe.wait_ge(xn_done, TT + t + 1)
                for h in range(2):
                    transposes(("fT", t, h), [xn[:, t, (4 * h + i) * P:(4 * h + i + 1) * P] for i in range(4)])
            wait_taken(pe, *all_of("fT"))
            name = ("logit",)
            wait_empty(pe, name)
            for t in range(TT):
                for k in range(KT):
                    last = mm(bank_of(name)[:, t * E:(t + 1) * E], hT[:, k, t * P:(t + 1) * P], wr[:, k, :],
                              start=(k == 0), stop=(k == KT - 1))
            last.then_inc(full(name), 1)
            name = ("rank",)
            pe.wait_ge(mask_done, 1)
            wait_empty(pe, name)
            rank = bank_of(name)
            mm(rank[:, 0:E], strict[:], mask[:, 0, :], start=True, stop=True)
            mm(rank[:, E:2 * E], strict[:], mask[:, 1, :], start=True, stop=False)
            mm(rank[:, E:2 * E], ones[:], mask[:, 0, :], start=False, stop=True)
            mm(rank[:, 2 * E:3 * E], ones[:], mask[:, 0, :], start=True, stop=False)
            mm(rank[:, 2 * E:3 * E], ones[:], mask[:, 1, :], start=False, stop=True).then_inc(full(name), 1)

            for b in range(BANKS):
                pe.wait_ge(drained[b], len([i for i in range(len(UNITS)) if i % BANKS == b]))

            def gather(wait):
                wait()
                for k in range(KT):
                    for t in range(TT):
                        last = mm(YB[:, k * SLOTS:(k + 1) * SLOTS], xn[:, t, k * P:(k + 1) * P], sel[:, t, :],
                                  start=(t == 0), stop=(t == TT - 1))
                last.then_inc(gathered, 1)

            def scatter(wait):
                wait()
                for t in range(TT):
                    for dh in range(2):
                        last = mm(ACC[t][dh][:, :], selgT[dh * SLOTS:(dh + 1) * SLOTS, t, :],
                                  y_sb[dh * SLOTS:(dh + 1) * SLOTS, :], start=False, stop=True, skip_group_check=True)
                return last

            def expert(j, more):
                pe.wait_ge(xg_done, j + (1 + more))
                for c in range(W1C):
                    pe.wait_ge(loaded[c], 16 * j + 16)
                    for bank, off in ((GLU, 0), (LIN, F)):
                        for dh in range(2):
                            last = mm(bank[dh * SLOTS:(dh + 1) * SLOTS, :], xgT[:, c, :],
                                      wring[:, c, off + dh * W:off + (dh + 1) * W], start=(c == 0), stop=False)
                    last.then_inc(chunk_used, 1)
                pe.wait_ge(aux_done, j + 1)
                for bank, off in ((GLU, 0), (LIN, F)):
                    for dh in range(2):
                        last = mm(bank[dh * SLOTS:(dh + 1) * SLOTS, :], esel, b1_all[:, off + dh * W:off + (dh + 1) * W],
                                  start=False, stop=True)
                last.then_inc(hid_filled, 1)

                def copied_out():
                    pe.wait_ge(y_copied, j + 1)
                    pe.wait_ge(selT_done, j + 1)

                scatter(copied_out)
                gather(lambda: pe.wait_ge(sel_done, j + (2 + more)))
                pe.wait_ge(actv_done, j + 1)
                for i in range(4):
                    last = nc.tensor.transpose(TB[:, i * P:(i + 1) * P], act_sb[:, i * P:(i + 1) * P], ident[:])
                last.then_inc(actT_filled, 1)
                pe.wait_ge(xg_done, j + (2 + more))
                pe.wait_ge(actT_done, j + 1)
                for c in range(W2C):
                    pe.wait_ge(loaded[W1C + c], 16 * j + 16)
                    for kk in range(2):
                        f = 2 * c + kk
                        for dh in range(2):
                            a = (f % 4) * P + (f // 4) * SLOTS
                            last = mm(YB[dh * SLOTS:(dh + 1) * SLOTS, :], actT[:, a:a + SLOTS],
                                      wring[:, W1C + c, kk * D + dh * W:kk * D + (dh + 1) * W],
                                      start=(f == 0), stop=(f == KT - 1))
                    last.then_inc(chunk_used, 1)
                for t in range(TT):
                    last = nc.tensor.transpose(TB[:, t * P:(t + 1) * P], selg[:, t, :], ident[:])
                last.then_inc(selT_filled, 1)

            pe.wait_ge(gate_done, 1)
            for t in range(TT):
                last = nc.tensor.transpose(TB[0:E, t * P:(t + 1) * P], gj[:, t, 0:E], ident[:])
            last.then_inc(gateT_filled, 1)
            pe.wait_ge(late_loaded, 16 * 3)
            gather(lambda: pe.wait_ge(sel_done, 1))
            pe.wait_ge(gateT_done, 1)
            for t in range(TT):
                for dh in range(2):
                    mm(ACC[t][dh][:, :], gateT[:, t * P:(t + 1) * P], b2_all[:, dh * W:(dh + 1) * W], start=True, stop=True)
            with pe.Fori(0, E) as j:
                expert(j, 0)

            pe.wait_ge(extra_done, 1)
            n = pe.value_load(n_extra[0:1, 0:1], min_val=0, max_val=OVF - 1)
            with pe.If(n > 0):
                pe.wait_ge(selT_done, E + 1)
                for t in range(TT):
                    last = mm(TB[0:E, 0:1], mask[:, t, :], ones[:, 0:1], start=(t == 0), stop=(t == TT - 1))
                last.then_inc(ovf_mm, 1)
                pe.wait_ge(ovf_dve, 1)
                mm(TB[0:E, 1:2], upper[0:E, 0:E], ecnt[:, 1:2], start=True, stop=True).then_inc(ovf_mm, 1)
                for t in range(TT):
                    last = nc.tensor.transpose(TB[0:E, P + t * P:P + (t + 1) * P], rj[:, t, 0:E], ident[:])
                last.then_inc(ovf_mm, 1)
                pe.wait_ge(ovf_dve, 3)
                for t in range(TT):
                    mm(TB[:, 384 + t * OVF:384 + (t + 1) * OVF], rankT[:, t * P:(t + 1) * P], onehot[:, E:E + OVF],
                       start=True, stop=True)
                    mm(TB[:, 416 + t * OVF:416 + (t + 1) * OVF], gateT[:, t * P:(t + 1) * P], onehot[:, E:E + OVF],
                       start=True, stop=True)
                mm(TB[0:1, 448:448 + OVF], row_id[:], onehot[:, E:E + OVF], start=True, stop=True).then_inc(ovf_mm, 1)
                pe.wait_ge(ovf_dve, 5)
                pe.wait_ge(y_copied, E + 1)
                gather(lambda: pe.wait_ge(sel_done, E + 2))
                with pe.Fori(0, n) as q:
                    expert(q + E, 1)
            pe.wait_ge(y_copied, n + (E + 1))
            pe.wait_ge(selT_done, n + (E + 1))
            scatter(lambda: None).then_inc(acc_done, 1)

            for t in range(TT):
                pe.wait_ge(xn_done, 2 * TT + t + 1)
                for h in range(2):
                    for i in range(4):
                        last = nc.tensor.transpose(banks[4 + 2 * t + h][:, i * P:(i + 1) * P],
                                                   xn[:, t, (4 * h + i) * P:(4 * h + i + 1) * P], ident[:])
                    last.then_inc(tail_filled, 1)
            pe.wait_ge(tail_hT, 4)
            for b in range(HALVES):
                for kh in range(2):
                    i = HALF_OF["pg", b, kh]
                    pe.wait_ge(blk_loaded[i % NB], 16 * (i // NB + 1))
                    for t in range(TT):
                        for kk in range(4):
                            k = 4 * kh + kk
                            last = mm(banks[2 * b + t][:, :], hT[:, k, t * P:(t + 1) * P],
                                      blk[:, i % NB, kk * W:(kk + 1) * W], start=(k == 0), stop=(k == KT - 1))
                        if kh == 1:
                            last.then_inc(tail_gate, 1)

        @block.scalar
        def _(act):
            fn = nc.scalar.activation

            def split(i):
                act.wait_ge(blk_loaded[i % NB], 16 * (i // NB + 1))
                fn(high(i), blk[:, i % NB, :], ACT.Copy).then_inc(blk_high, 1)

            def square_sums(wait, n, junk):
                for t in range(TT):
                    wait(t)
                    fn(junk[:, t, :], x[:, t, :], ACT.Square, accum_out=ssq[:, t:t + 1]).then_inc(ssq_done, 1)
                act.wait_ge(ms_done, n + 1)
                fn(rstd[:], ssq[:], ACT.Sqrt).then_inc(rstd_done, 1)

            square_sums(lambda t: act.wait_ge(x_loaded[t], 16), 0, u)

            def taps(b, j):
                name = ("xbc", b, j)
                wait_filled(act, name)
                for c in range(2):
                    ct = 4 * b + 2 * j + c
                    wcol = ROWS["conv_w"] + (TAPS - 1) * CONV_TILES + ct
                    last = fn(xbcT[:, ct, :], bank_of(name)[:, c * TOKENS:(c + 1) * TOKENS], ACT.Identity,
                              bias=paramT[:, ROWS["conv_b"] + ct:ROWS["conv_b"] + ct + 1], scale=paramT[:, wcol:wcol + 1])
                last.then_inc(tap_done, 1)

            def conv_sigmoid(b, j):
                act.wait_ge(conv_done, 2 * b + j + 1)
                ct = 4 * b + 2 * j
                fn(bank_of(("xbc", b, j))[:, :], xbcT[:, ct:ct + 2, :].rearrange("p c t -> p (c t)"),
                   ACT.Sigmoid).then_inc(sig_done, 1)

            split(0)
            split(1)
            for t in range(TT):
                for h in range(2):
                    wait_taken(act, ("xT", t, h))
                    cols = (slice(None), slice(4 * h, 4 * h + 4), slice(t * P, (t + 1) * P))
                    fn(a_hi[cols], hT[cols], ACT.Copy).then_inc(act_high, 1)
            split(2)
            split(3)
            act.wait_ge(small_loaded, 16 * 6)
            fn(wdt_hi[:], wdt.rearrange("p k h -> p (k h)"), ACT.Copy).then_inc(wdt_high, 1)
            wait_taken(act, ("param",))
            order = [(b, j) for b in range(4) for j in range(2)]
            for i, bj in enumerate(order):
                if i:
                    split(i + 3)
                taps(*bj)
                if i:
                    conv_sigmoid(*order[i - 1])
            conv_sigmoid(*order[-1])
            act.wait_ge(dt_neg, 1)
            fn(dtx[:, 2], dtx[:, 1], ACT.Exp).then_inc(dt_exp, 1)
            fn(alog[:], alog[:], ACT.Exp)
            act.wait_ge(dt_one, 1)
            fn(dtx[:, 4], dtx[:, 3], ACT.Ln).then_inc(dt_ln, 1)

            def split_ahead(kind, b):
                for kh in range(2):
                    i = HALF_OF[kind, b, kh] + NB - 1
                    if i < SPLIT:
                        split(i)

            def natural(kind, func, dst):
                for b in range(HALVES):
                    if kind in NATURAL:
                        split_ahead(kind, b)
                    for t in range(TT):
                        wait_filled(act, (kind, b, t))
                        fn(dst[:, t, b * W:(b + 1) * W], bank_of((kind, b, t))[:, :], func).then_inc(empty((kind, b, t)), 1)

            def high_parts(kind, dst):
                for t in range(TT):
                    for h in range(2):
                        name = (kind, t, h)
                        wait_filled(act, name)
                        fn(dst[:, 4 * h:4 * h + 4, t * P:(t + 1) * P], seg4(bank_of(name)[:, :]),
                           ACT.Copy).then_inc(act_high, 1)

            def copy(name, dst, src=None):
                wait_filled(act, name)
                fn(dst, bank_of(name)[:, :] if src is None else src, ACT.Copy).then_inc(empty(name), 1)

            natural("v", ACT.Gelu, v)
            for c in range(TT):
                for h in range(2):
                    copy(("xs", c, h), xs[:, c, h * W:(h + 1) * W])
            copy(("bn",), bnat.rearrange("p g n -> p (g n)"))
            act.wait_ge(acs_done, 1)
            fn(edec[:], acs[:], ACT.Exp).then_inc(edec_done, 1)
            act.wait_ge(v_var, 1)
            fn(rstd[:], ssq[:], ACT.Sqrt).then_inc(v_rstd, 1)
            natural("u", ACT.Gelu, u)
            for c in range(TT):
                for g in range(GROUPS):
                    wait_taken(act, ("seg", c, g))
                    d = decay[c][:, g * HPG:(g + 1) * HPG, :]
                    fn(d, d, ACT.Exp).then_inc(dexp_done, 1)
            for b in range(HALVES):
                split_ahead("z", b)
                for t in range(TT):
                    wait_filled(act, ("z", b, t))
                    fn(z[:, t, b * W:(b + 1) * W], bank_of(("z", b, t))[:, :], ACT.Sigmoid).then_inc(zsig_done, 1)
            for h in range(2):
                copy(("state", h), state[:, h * W:(h + 1) * W])
            split_ahead("ga", 0)
            for t in range(TT):
                act.wait_ge(y_done, t + 1)
                for g in range(GROUPS):
                    last = fn(xbcT[:, t * GROUPS + g, :], z[:, t, g * GDIM:(g + 1) * GDIM], ACT.Square,
                              accum_out=yssq[:, t, g:g + 1])
                last.then_inc(yssq_done, 1)
            act.wait_ge(yms_done, 1)
            fn(yssq[:], yssq[:], ACT.Sqrt).then_inc(yrstd_done, 1)
            for b in range(HALVES):
                if b:
                    split_ahead("ga", b)
                for t in range(TT):
                    name = ("ga", b, t)
                    wait_filled(act, name)
                    fn(ga[:, t, b * W:(b + 1) * W], bank_of(name)[:, :], ACT.Sigmoid).then_inc(empty(name), 1)
            high_parts("yaT", b_hi)
            natural("gb", ACT.Sigmoid, gb)
            split_ahead("wa", 0)
            wait_filled(act, ("gb", 1, 1))
            for t in range(TT):
                for h in range(2):
                    wait_taken(act, ("ybT", t, h))
                    cols = (slice(None), slice(4 * h, 4 * h + 4), slice(t * P, (t + 1) * P))
                    fn(a_hi[cols], ybT[cols], ACT.Copy).then_inc(act_high, 1)
            split_ahead("wa", 1)
            split_ahead("wb", 0)
            split_ahead("wb", 1)

            def embed(b):
                for t in range(TT):
                    copy(("pp", b, t), yproj[:, t, b * W:(b + 1) * W])

            copy(("pT",), pT, bank_of(("pT",))[:, :].rearrange("p (k t) -> p k t", k=2))
            split_ahead("wo", 0)
            embed(0)
            high_parts("mT", b_hi)
            square_sums(lambda t: wait_taken(act, ("wo", 0, t), ("wo", 1, t)), 1, junk)
            embed(1)
            act.wait_ge(neg_max, 1)
            for t in range(TT):
                last = fn(ex[:, t, :], lg[:, t, 0:E], ACT.Exp, bias=ngm[:, t:t + 1])
            last.then_inc(lexp_done, 1)

            def expert(j):
                act.wait_ge(g_done, j + 1)
                fn(sig_sb, g_sb, ACT.Sigmoid, scale=ALPHA).then_inc(msig_done, 1)
                act.wait_ge(chunk_used, NCH * j + NCH)
                fn(y_sb, YB[:, :], ACT.Copy).then_inc(y_copied, 1)

            with act.Fori(0, E) as j:
                expert(j)
            act.wait_ge(extra_done, 1)
            n = act.value_load(n_extra[0:1, 0:1], min_val=0, max_val=OVF - 1)
            with act.If(n > 0):
                with act.Fori(0, n) as q:
                    expert(q + E)

            square_sums(lambda t: act.wait_ge(x2_done, t + 1), 2, junk)
            for b in range(HALVES):
                for t in range(TT):
                    act.wait_ge(tail_gate, 2 * b + t + 1)
                    fn(v[:, t, b * W:(b + 1) * W], banks[2 * b + t][:, :], ACT.Sigmoid).then_inc(tail_sig, 1)
            square_sums(lambda t: act.wait_ge(x3_done, t + 1), 3, junk)

        @block.vector
        def _(dve):
            ts, tt, stt = nc.vector.tensor_scalar, nc.vector.tensor_tensor, nc.vector.scalar_tensor_tensor
            cp = nc.vector.tensor_copy
            steps = [0]

            def link(ins):
                steps[0] += 1
                ins.then_inc(dve_step, 1)
                dve.wait_ge(dve_step, steps[0])

            def norm(n, dst, wait=None):
                dve.wait_ge(ssq_done, TT * (n + 1))
                link(ts(ssq[:], ssq[:], 1.0 / D, RMS_EPS, ALU.mult, ALU.add))
                nc.vector.reciprocal(ssq[:], ssq[:]).then_inc(ms_done, 1)
                dve.wait_ge(rstd_done, n + 1)
                if dst is not None:
                    for t in range(TT):
                        ts(dst[:, t, :], x[:, t, :], rstd[:, t:t + 1], None, ALU.mult).then_inc(xn_done, 1)

            def scaled(name, dst, row, t, h, done=None):
                gain = paramT[:, row + 4 * h:row + 4 * h + 4].unsqueeze(2).to_broadcast([P, 4, P])
                wait_filled(dve, name)
                tt(dst[:, 4 * h:4 * h + 4, t * P:(t + 1) * P], seg4(bank_of(name)[:, :]), gain, ALU.mult).then_inc(empty(name), 1)

            osteps = [0]

            def olink(ins):
                osteps[0] += 1
                ins.then_inc(ovf_step, 1)
                dve.wait_ge(ovf_step, osteps[0])

            norm(0, v)
            wait_filled(dve, ("param",))
            cp(paramT[:], bank_of(("param",))[:, 0:NROWS]).then_inc(empty(("param",)), 1)
            wait_taken(dve, ("param",))
            for t in range(TT):
                for h in range(2):
                    scaled(("xT", t, h), hT, ROWS["mix"], t, h)

            def low_parts(kind, raw, hi, lo, n):
                for t in range(TT):
                    for h in range(2):
                        n += 1
                        dve.wait_ge(act_high, n)
                        cols = (slice(None), slice(4 * h, 4 * h + 4), slice(t * P, (t + 1) * P))
                        if raw is not None:
                            tt(lo[cols], raw[cols], hi[cols].bitcast(FP32), ALU.subtract).then_inc(act_low, 1)
                        else:
                            name = (kind, t, h)
                            tt(lo[cols], seg4(bank_of(name)[:, :]), hi[cols].bitcast(FP32),
                               ALU.subtract).then_inc(empty(name), 1)

            low_parts("xT", hT, a_hi, a_lo, 0)

            def conv(b, j, n):
                name = ("xbc", b, j)
                dve.wait_ge(tap_done, n + 1)
                for s in range(1, TAPS):
                    for c in range(2):
                        ct = 4 * b + 2 * j + c
                        w = ROWS["conv_w"] + (TAPS - 1 - s) * CONV_TILES + ct
                        last = stt(xbcT[:, ct, s:], bank_of(name)[:, c * TOKENS:(c + 1) * TOKENS - s], paramT[:, w:w + 1],
                                   xbcT[:, ct, s:], ALU.mult, ALU.add)
                    if s < TAPS - 1:
                        link(last)
                last.then_inc(conv_done, 1)

            def conv_silu(b, j, n):
                name = ("xbc", b, j)
                dve.wait_ge(sig_done, n + 1)
                ct = 4 * b + 2 * j
                both = xbcT[:, ct:ct + 2, :].rearrange("p c t -> p (c t)")
                tt(both, both, bank_of(name)[:, :], ALU.mult).then_inc(empty(name), 1)

            order = [(b, j) for b in range(4) for j in range(2)]
            for i, bj in enumerate(order):
                conv(*bj, i)
                if i:
                    conv_silu(*order[i - 1], i - 1)
            conv_silu(*order[-1], len(order) - 1)

            raw, neg, e_, one, log_, tmp = (dtx[:, i] for i in range(6))
            dve.wait_ge(small_loaded, 16 * 6)
            wait_filled(dve, ("dt",))
            link(tt(raw, bank_of(("dt",))[:, 0:TT * HEADS].rearrange("p (t h) -> p t h", t=TT),
                    dtb[:].unsqueeze(1).to_broadcast([P, TT, HEADS]), ALU.add))
            stt(neg, raw, -1.0, raw, ALU.mult, ALU.min).then_inc(dt_neg, 1)
            dve.wait_ge(dt_exp, 1)
            ts(one, e_, 1.0, None, ALU.add).then_inc(dt_one, 1)
            dve.wait_ge(dt_one, 1)
            link(stt(tmp, one, -1.0, e_, ALU.add, ALU.subtract))
            link(nc.vector.reciprocal(neg, one))
            link(tt(tmp, tmp, neg, ALU.mult))
            dve.wait_ge(dt_ln, 1)
            link(tt(log_, log_, tmp, ALU.subtract))
            link(stt(dt[:], raw, 0.0, log_, ALU.max, ALU.add))
            stt(adt[:], dt[:], -1.0, alog[:].unsqueeze(1).to_broadcast([P, TT, HEADS]), ALU.mult, ALU.mult).then_inc(adt_done, 1)
            dve.wait_ge(adt_done, 1)
            cp(dtx[:, 5], dtx[:, 0]).then_inc(empty(("dt",)), 1)

            for b in range(HALVES):
                for t in range(TT):
                    wait_taken(dve, ("v", b, t))
                    last = nc.vector.bn_stats(vstat[:, t, b, :], v[:, t, b * W:(b + 1) * W])
            link(last)
            for t in range(TT):
                last = nc.vector.bn_aggr(vmean[:, t, :], vstat[:, t].rearrange("p a b -> p (a b)"))
            link(last)
            link(ts(ssq[:], vmean[:, :, 1], LN_EPS, None, ALU.add))
            nc.vector.reciprocal(ssq[:], ssq[:]).then_inc(v_var, 1)
            link(nc.vector.memset(sgu_wT[CHUNK:P, :, 0:CHUNK], 0.0))
            for h in range(2):
                name = ("sguw", h)
                wait_filled(dve, name)
                cp(sgu_wT[0:CHUNK, 4 * h:4 * h + 4, :], seg4(bank_of(name)[0:CHUNK, :]))
                cp(sgu_wT[CHUNK:P, 4 * h:4 * h + 4, CHUNK:P], seg4(bank_of(name)[CHUNK:P, :])[:, :, CHUNK:P]).then_inc(empty(name), 1)
            name = ("acs",)
            wait_filled(dve, name)
            both = bank_of(name)[:, 0:TT * 2 * HEADS].rearrange("p (c a h) -> p c a h", c=TT, a=2)
            link(cp(acs[:, :, 0, :], both[:, :, 0, :]))
            tt(acs[:, :, 1, :], both[:, :, 1, :], acs[:, :, 0, :], ALU.subtract).then_inc(acs_done, 1)
            dve.wait_ge(acs_done, 1)
            cp(dtx[:, 5], dtx[:, 0]).then_inc(empty(name), 1)

            def heads(ap):
                return ap.rearrange("p (h n) -> p h n", n=HEAD_DIM)

            def per_head(ap):
                return ap.unsqueeze(2).to_broadcast([P, ap.shape[1], HEAD_DIM])

            for c in range(TT):
                wait_taken(dve, ("xs", c, 0), ("xs", c, 1))
                tt(heads(xdt[:, c, :]), heads(xs[:, c, :]), per_head(dt[:, c, :]), ALU.mult).then_inc(xdt_done, 1)
            dve.wait_ge(edec_done, 1)
            dve.wait_ge(xdt_done, TT)
            tt(heads(xdte), heads(xdt[:, 0, :]), per_head(edec[:, 0, 1, :]), ALU.mult).then_inc(xdt_done, 1)
            for c in range(TT):
                tt(heads(xs[:, c, :]), heads(xs[:, c, :]), per_head(dskip[:]), ALU.mult)
            dve.wait_ge(v_rstd, 1)
            dve.wait_ge(ln_loaded, 32)
            for t in range(TT):
                last = ts(v[:, t, :], v[:, t, :], vmean[:, t, 0:1], rstd[:, t:t + 1], ALU.subtract, ALU.mult)
            link(last)
            for t in range(TT):
                last = tt(v[:, t, :], v[:, t, :], ln_g, ALU.mult)
            link(last)
            for t in range(TT):
                tt(v[:, t, :], v[:, t, :], ln_b, ALU.add).then_inc(v_done, 1)
            for c in range(TT):
                name = ("cb", c)
                wait_filled(dve, name)
                tt(cbm[:, c], seg4(bank_of(name)[:, :]), upper[:].unsqueeze(1).to_broadcast([P, GROUPS, P]),
                   ALU.mult).then_inc(empty(name), 1)
            wait_taken(dve, *all_of("u"))
            for c in range(TT):
                for h in range(2):
                    name = ("mix", c, h)
                    wait_filled(dve, name)
                    for i in range(4):
                        g = 4 * h + i
                        r = ROWS["sgu_b"] + g
                        cols = u[:, c, g * P:(g + 1) * P]
                        last = stt(cols, bank_of(name)[:, i * P:(i + 1) * P], paramT[:, r:r + 1], cols, ALU.add, ALU.mult)
                    last.then_inc(empty(name), 1)

            def segments(c, g):
                name = ("seg", c, g)
                wait_filled(dve, name)
                for r in range(HPG):
                    h = g * HPG + r
                    last = ts(decay[c][:, h, :], bank_of(name)[:, r * P:(r + 1) * P], acs[:, c, 0, h:h + 1], 0.0,
                              ALU.subtract, ALU.min)
                last.then_inc(empty(name), 1)

            def decays(c, g, n):
                dve.wait_ge(dexp_done, n + 1)
                d = decay[c][:, g * HPG:(g + 1) * HPG, :]
                tt(d, d, cbm[:, c, g, :].unsqueeze(1).to_broadcast([P, HPG, P]), ALU.mult).then_inc(decay_done, 1)

            wait_taken(dve, ("cb", 0), ("cb", 1))
            order = [(c, g) for c in range(TT) for g in range(GROUPS)]
            for i, cg in enumerate(order):
                segments(*cg)
                if i >= 2:
                    decays(*order[i - 2], i - 2)
            for i in (-2, -1):
                decays(*order[i], len(order) + i)
            for i, name in enumerate(all_of("z")):
                _, b, t = name
                dve.wait_ge(zsig_done, i + 1)
                cols = z[:, t, b * W:(b + 1) * W]
                tt(cols, cols, bank_of(name)[:, :], ALU.mult).then_inc(empty(name), 1)
            wait_taken(dve, *all_of("z"))

            def y_take(c, hf):
                name = ("yd", c, hf)
                cols = xs[:, c, hf * W:(hf + 1) * W]
                wait_filled(dve, name)
                tt(cols, cols, bank_of(name)[:, :], ALU.add).then_inc(empty(name), 1)
                wait_taken(dve, name)
                if c:
                    off = ("yo", hf)
                    tmp = xdte[:, hf * W:(hf + 1) * W]
                    wait_filled(dve, off)
                    tt(heads(tmp), heads(bank_of(off)[:, :]), per_head(edec[:, 1, 0, 8 * hf:8 * hf + 8]), ALU.mult).then_inc(empty(off), 1)
                    wait_taken(dve, off)
                    link(tt(cols, cols, tmp, ALU.add))

            for c in range(TT):
                for hf in range(2):
                    y_take(c, hf)
                tt(z[:, c, :], z[:, c, :], xs[:, c, :], ALU.mult).then_inc(y_done, 1)
            dve.wait_ge(yssq_done, TT)
            link(ts(yssq[:], yssq[:], 1.0 / GDIM, RMS_EPS, ALU.mult, ALU.add))
            nc.vector.reciprocal(yssq[:], yssq[:]).then_inc(yms_done, 1)
            dve.wait_ge(yrstd_done, 1)
            for t in range(TT):
                zg = z[:, t, :].rearrange("p (g n) -> p g n", g=GROUPS)
                tt(zg, zg, yssq[:, t, :].unsqueeze(2).to_broadcast([P, GROUPS, GDIM]), ALU.mult).then_inc(yb_done, 1)

            low_parts("yaT", None, b_hi, b_lo, 4)
            wait_taken(dve, *all_of("ga"), *all_of("gb"))

            def gate_a(b):
                for t in range(TT):
                    name = ("wa", b, t)
                    cols = ga[:, t, b * W:(b + 1) * W]
                    wait_filled(dve, name)
                    tt(cols, cols, bank_of(name)[:, :], ALU.mult).then_inc(empty(name), 1)

            gate_a(0)
            for t in range(TT):
                for h in range(2):
                    scaled(("ybT", t, h), ybT, ROWS["ssm"], t, h)
            low_parts("ybT", ybT, a_hi, a_lo, 8)
            gate_a(1)
            wait_taken(dve, *all_of("wa"))
            for name in all_of("wb"):
                _, b, t = name
                cols = slice(b * W, (b + 1) * W)
                wait_filled(dve, name)
                tt(gb[:, t, cols], gb[:, t, cols], bank_of(name)[:, :], ALU.mult).then_inc(empty(name), 1)
                wait_taken(dve, name)
                tt(ga[:, t, cols], ga[:, t, cols], gb[:, t, cols], ALU.add).then_inc(merged, 1)
            low_parts("mT", None, b_hi, b_lo, 12)
            dve.wait_ge(x_reloaded, 16 * TT)
            for name in all_of("wo"):
                _, b, t = name
                cols = x[:, t, b * W:(b + 1) * W]
                wait_filled(dve, name)
                tt(cols, cols, bank_of(name)[:, :], ALU.add).then_inc(empty(name), 1)

            norm(1, xn)
            for t in range(TT):
                for h in range(2):
                    scaled(("fT", t, h), hT, ROWS["ffn"], t, h)

            name = ("logit",)
            wait_filled(dve, name)
            nc.vector.memset(lg[:, :, E:E + 4], BIG)
            nc.vector.memset(rep[:, :, TOPK:8], BIG)
            tt(lg[:, :, 0:E], bank_of(name)[:, 0:TT * E].rearrange("p (t e) -> p t e", t=TT),
               br[:].unsqueeze(1).to_broadcast([P, TT, E]), ALU.add).then_inc(empty(name), 1)
            wait_taken(dve, name)
            for t in range(TT):
                last = nc.vector.max(top[:, t, :], lg[:, t, 0:E])
            link(last)
            ts(ngm, top[:, :, 0], -1.0, None, ALU.mult).then_inc(neg_max, 1)
            link(cp(rep[:, :, 0:TOPK], top[:, :, 0:TOPK]))
            for t in range(TT):
                last = nc.vector.match_replace(lg2[:, t, :], rep[:, t, :], lg[:, t, :], -BIG)
            link(last)
            tt(mask, lg2[:, :, 0:E], lg[:, :, 0:E], ALU.not_equal).then_inc(mask_done, 1)
            nc.vector.memset(rj[:, :, E:NJ], -1.0)
            cp(onehot[:, 0:E], ident[0:E, 0:E])
            dve.wait_ge(mask_done, 1)
            dve.wait_ge(lexp_done, 1)
            link(tt(ex, ex, mask, ALU.mult))
            link(nc.vector.reduce_sum(gsum, ex, AX.X))
            link(nc.vector.reciprocal(gsum, gsum))
            tt(gj[:, :, 0:E], ex, gsum.unsqueeze(2).to_broadcast([P, TT, E]), ALU.mult).then_inc(gate_done, 1)
            name = ("rank",)
            wait_filled(dve, name)
            rank = bank_of(name)
            link(stt(rj[:, :, 0:E], rank[:, 0:TT * E].rearrange("p (t e) -> p t e", t=TT), 1.0, mask, ALU.add, ALU.mult))
            link(ts(rj[:, :, 0:E], rj[:, :, 0:E], -1.0, None, ALU.add))

            def select(j):
                for t in range(TT):
                    last = ts(sel[:, t, :], slot_id[:, 0:SLOTS], rj[:, t, bass.ds(j, 1)], None, ALU.is_equal)
                last.then_inc(sel_done, 1)

            def take_gathered():
                tt(xgT, YB[:, :].rearrange("p (k s) -> p k s", k=KT),
                   paramT[:, ROWS["ffn"]:ROWS["ffn"] + KT].unsqueeze(2).to_broadcast([P, KT, SLOTS]), ALU.mult).then_inc(xg_done, 1)

            select(0)
            link(cp(cnt, rank[0:1, 2 * E:3 * E]))
            link(ts(cov, cnt, float(SLOTS), None, ALU.is_gt))
            for m in (2, 3):
                link(stt(cov, cnt, float(m * SLOTS), cov, ALU.is_gt, ALU.add))
            link(nc.vector.reduce_sum(cnt[:, 0:1], cov, AX.X))
            cp(n_extra[:], cnt[:, 0:1]).then_inc(extra_done, 1)
            nc.vector.memset(selgT, 0.0).then_inc(selT_done, 1)
            wait_taken(dve, ("pT",))
            nc.vector.memset(y_sb, 0.0).then_inc(y_copied, 1)
            cp(dtx[:, 5], dtx[:, 0]).then_inc(empty(("rank",)), 1)
            dve.wait_ge(gateT_filled, 1)
            cp(gateT, TB[0:E, 0:TOKENS]).then_inc(gateT_done, 1)
            dve.wait_ge(gathered, 1)
            take_gathered()

            def expert(j, more):
                select(j + 1)
                ts(esel, ones[0:E, 0:SLOTS], onehot[:, bass.ds(j, 1)], None, ALU.mult)
                for t in range(TT):
                    last = ts(selg[:, t, :], slot_id[:], rj[:, t, bass.ds(j, 1)], gj[:, t, bass.ds(j, 1)],
                              ALU.is_equal, ALU.mult)
                last.then_inc(aux_done, 1)
                dve.wait_ge(hid_filled, j + 1)
                ts(g_sb, GLU[:, :], LIMIT, None, ALU.min).then_inc(g_done, 1)
                ts(lin_sb, LIN[:, :], LIMIT, -LIMIT, ALU.min, ALU.max).then_inc(loop_step, 1)
                dve.wait_ge(loop_step, 2 * j + 1)
                stt(act_sb, lin_sb, 1.0, g_sb, ALU.add, ALU.mult).then_inc(loop_step, 1)
                dve.wait_ge(loop_step, 2 * j + 2)
                dve.wait_ge(msig_done, j + 1)
                tt(act_sb, act_sb, sig_sb, ALU.mult).then_inc(actv_done, 1)
                dve.wait_ge(gathered, j + (2 + more))
                take_gathered()
                dve.wait_ge(actT_filled, j + 1)
                cp(actT, TB[:, :]).then_inc(actT_done, 1)
                dve.wait_ge(selT_filled, j + 1)
                cp(selgT.rearrange("p t s -> p (t s)"), TB[:, 0:TT * P]).then_inc(selT_done, 1)

            with dve.Fori(0, E) as j:
                expert(j, 0)
            n = dve.value_load(n_extra[0:1, 0:1], min_val=0, max_val=OVF - 1)
            with dve.If(n > 0):
                dve.wait_ge(ovf_mm, 1)
                olink(cp(ecnt[:, 0:1], TB[0:E, 0:1]))
                olink(ts(ecnt[:, 1:2], ecnt[:, 0:1], float(SLOTS), None, ALU.is_gt))
                olink(stt(ecnt[:, 1:2], ecnt[:, 0:1], 2.0 * SLOTS, ecnt[:, 1:2], ALU.is_gt, ALU.add))
                stt(ecnt[:, 1:2], ecnt[:, 0:1], 3.0 * SLOTS, ecnt[:, 1:2], ALU.is_gt, ALU.add).then_inc(ovf_dve, 1)
                dve.wait_ge(ovf_mm, 3)
                dve.wait_ge(ovf_dve, 1)
                olink(cp(ecnt[:, 2:3], TB[0:E, 1:2]))
                olink(tt(estart, ecnt[:, 2:3], ecnt[:, 1:2], ALU.subtract))
                olink(ts(ecnt[:, 3:4], estart, float(SLOTS), None, ALU.mult))
                olink(ts(ohtmp, slot_id[0:E, 0:OVF], estart, None, ALU.is_ge))
                stt(onehot[:, E:E + OVF], slot_id[0:E, 0:OVF], ecnt[:, 2:3], ohtmp, ALU.is_lt, ALU.mult).then_inc(ovf_dve, 1)
                ts(rankT, TB[0:E, P:P + TOKENS], ecnt[:, 3:4], None, ALU.add).then_inc(ovf_dve, 1)
                olink(ts(ofs, slot_id[:, 0:OVF], -float(SLOTS), -float(SLOTS), ALU.mult, ALU.add))
                dve.wait_ge(ovf_mm, 4)
                for t in range(TT):
                    tt(rj[:, t, E:E + OVF], TB[:, 384 + t * OVF:384 + (t + 1) * OVF], ofs, ALU.add)
                    last = cp(gj[:, t, E:E + OVF], TB[:, 416 + t * OVF:416 + (t + 1) * OVF])
                last.then_inc(ovf_dve, 1)
                cp(ids[:], TB[0:1, 448:448 + OVF]).then_inc(ovf_dve, 1)
                dve.wait_ge(ovf_dve, 5)
                select(E)
                dve.wait_ge(gathered, E + 2)
                take_gathered()
                with dve.Fori(0, n) as q:
                    expert(q + E, 1)

            dve.wait_ge(acc_done, 1)
            for t in range(TT):
                for dh in range(2):
                    cols = x[:, t, dh * W:(dh + 1) * W]
                    last = tt(cols, cols, ACC[t][dh][:, :], ALU.add)
                last.then_inc(x2_done, 1)
            norm(2, xn)
            for t in range(TT):
                for h in range(2):
                    gain = paramT[:, ROWS["ple"] + 4 * h:ROWS["ple"] + 4 * h + 4].unsqueeze(2).to_broadcast([P, 4, P])
                    dve.wait_ge(tail_filled, 2 * t + h + 1)
                    tt(hT[:, 4 * h:4 * h + 4, t * P:(t + 1) * P], seg4(banks[4 + 2 * t + h][:, :]), gain, ALU.mult).then_inc(tail_hT, 1)
            for b in range(HALVES):
                for t in range(TT):
                    cols = slice(b * W, (b + 1) * W)
                    dve.wait_ge(tail_sig, 2 * b + t + 1)
                    link(tt(v[:, t, cols], v[:, t, cols], yproj[:, t, cols], ALU.mult))
                    last = tt(x[:, t, cols], x[:, t, cols], v[:, t, cols], ALU.add)
                    if b == HALVES - 1:
                        last.then_inc(x3_done, 1)
            norm(3, None)
            for t in range(TT):
                stt(xn[:, t, :], x[:, t, :], rstd[:, t:t + 1], fnorm, ALU.mult, ALU.mult).then_inc(out_ready, 1)


_INS = ["x", "p", "mix_norm", "w_in", "sgu_ln_g", "sgu_ln_b", "sgu_w", "sgu_b", "conv_w", "conv_b", "dt_bias", "a_log",
        "d_skip", "ssm_norm", "w_branch_a", "w_branch_b", "w_out", "ffn_norm", "w_router", "b_router", "w1", "b1", "w2",
        "b2", "ple_norm", "w_ple_gate", "w_ple_proj", "final_norm"]
_OUTS = [((1, TOKENS, D), "float32")]


def kernel(**inputs):
    import numpy as _np
    import concourse.bacc as _bacc
    from concourse import mybir as _mybir
    from concourse.bass_utils import run_bass_kernel_spmd as _run

    nc = _bacc.Bacc("TRN2", target_bir_lowering=False, num_devices=1)
    arrays, args = {}, []
    for name in _INS:
        a = _np.ascontiguousarray(inputs[name])
        arrays[f"in_{name}_dram"] = a
        args.append(nc.dram_tensor(f"in_{name}_dram", a.shape, _mybir.dt.from_np(a.dtype), kind="ExternalInput").ap())
    for i, (shape, dtype) in enumerate(_OUTS):
        dt = _mybir.dt.from_np(_np.dtype(dtype))
        args.append(nc.dram_tensor(f"out_{i}_dram", shape, dt, kind="ExternalOutput").ap())
    build(nc, *args)
    r = _run(nc, [arrays], core_ids=[0])
    return r.results[0]["out_0_dram"]
```
